# Optimizing a Trainium2 kernel written in Bass

```python
import math
import jax, jax.numpy as jnp
from jax import lax
import numpy as np

D_MODEL = 1024
BATCH = 1
SEQ = 256
DEPTH = 2

GRID_W = 64
NA_HEADS = 8
NA_HEAD_DIM = 64
NA_WIDTH = NA_HEADS * NA_HEAD_DIM
NA_WIN_ROWS = 8
NA_WIN_COLS = 16
NA_COL_BLOCK = NA_WIN_COLS
NA_KEY_COL_BLOCK = 2 * NA_WIN_COLS
DIFF_HEADS = 4
DIFF_HEAD_DIM = 64
DIFF_QK_WIDTH = DIFF_HEADS * 2 * DIFF_HEAD_DIM
DIFF_V_WIDTH = DIFF_HEADS * 2 * DIFF_HEAD_DIM
MLA_HEADS = 8
MLA_NOPE_DIM = 64
MLA_ROPE_DIM = 32
MLA_V_DIM = 64
MLA_Q_RANK = 384
MLA_KV_RANK = 256
MLA_WIDTH = MLA_HEADS * MLA_V_DIM
N_BRANCH = 3
BRANCH_WIDTH = 512
D_IN = 3 * NA_WIDTH + 2 * DIFF_QK_WIDTH + DIFF_V_WIDTH + MLA_Q_RANK + MLA_KV_RANK + MLA_ROPE_DIM + N_BRANCH * D_MODEL
D_FF = -(-8 * D_MODEL // (3 * 256)) * 256
ROPE_THETA = 500000.0
DIFF_ROT_DIM = DIFF_HEAD_DIM // 4
Q_BLOCK = 128
DN_ALPHA = (2 * DEPTH) ** 0.25
DN_BETA = (8 * DEPTH) ** -0.25
LN_EPS = 1e-5
RMS_EPS = 1e-6


def layer_norm(x, g, b):
    xf = x.astype(jnp.float32)
    mu = jnp.mean(xf, -1, keepdims=True)
    var = jnp.mean(jnp.square(xf - mu), -1, keepdims=True)
    return ((xf - mu) * lax.rsqrt(var + LN_EPS) * g.astype(jnp.float32) + b.astype(jnp.float32)).astype(x.dtype)

def rms_norm(x, g):
    xf = x.astype(jnp.float32)
    return (xf * lax.rsqrt(jnp.mean(xf * xf, -1, keepdims=True) + RMS_EPS) * g.astype(jnp.float32)).astype(x.dtype)

def rope(x, rot_dim):
    s = x.shape[1]
    half = rot_dim // 2
    inv_freq = jnp.exp(-math.log(ROPE_THETA) * jnp.arange(half, dtype=jnp.float32) / half)
    ang = jnp.arange(s, dtype=jnp.float32)[:, None] * inv_freq[None, :]
    cos = jnp.cos(ang)[None, :, None, :]
    sin = jnp.sin(ang)[None, :, None, :]
    xr = x[..., :rot_dim].astype(jnp.float32)
    x1, x2 = xr[..., :half], xr[..., half:]
    rot = jnp.concatenate([x1 * cos - x2 * sin, x2 * cos + x1 * sin], -1).astype(x.dtype)
    return jnp.concatenate([rot, x[..., rot_dim:]], -1)

def blocked_attention(q, k, v, scale):
    b, s, h, dq = q.shape
    nb = s // Q_BLOCK
    qb = q.reshape(b, nb, Q_BLOCK, h, dq).transpose(1, 0, 2, 3, 4)

    def one_block(qi):
        sc = jnp.einsum('bqhd,bkhd->bhqk', qi, k, preferred_element_type=jnp.float32) * scale
        p = jax.nn.softmax(sc, axis=-1).astype(v.dtype)
        return jnp.einsum('bhqk,bkhd->bqhd', p, v)

    out = lax.map(one_block, qb)
    return out.transpose(1, 0, 2, 3, 4).reshape(b, s, h, v.shape[-1])

def neighbourhood_attention(q, k, v, rpb):
    b, s, h, d = q.shape
    rows = s // GRID_W
    kr = min(NA_WIN_ROWS, rows)
    kc = NA_WIN_COLS
    ncb = GRID_W // NA_COL_BLOCK
    qg = q.reshape(b, rows, GRID_W, h, d)
    kg = k.reshape(b, rows, GRID_W, h, d)
    vg = v.reshape(b, rows, GRID_W, h, d)
    qcol = jnp.arange(GRID_W).reshape(ncb, NA_COL_BLOCK)
    kstart = jnp.clip(jnp.arange(ncb) * NA_COL_BLOCK - kc // 2, 0, GRID_W - NA_KEY_COL_BLOCK)
    kcol = kstart[:, None] + jnp.arange(NA_KEY_COL_BLOCK)[None, :]
    wstart = jnp.clip(qcol - kc // 2, 0, GRID_W - kc)
    col_valid = (kcol[:, None, :] >= wstart[:, :, None]) & (kcol[:, None, :] < wstart[:, :, None] + kc)
    dcol_idx = jnp.clip(kcol[:, None, :] - qcol[:, :, None], -(kc - 1), kc - 1) + (kc - 1)
    row_center = NA_WIN_ROWS - 1
    scale = d ** -0.5

    def one_row(r):
        rs = jnp.clip(r - kr // 2, 0, rows - kr)
        qr = lax.dynamic_index_in_dim(qg, r, axis=1, keepdims=False)
        k_rows = lax.dynamic_slice_in_dim(kg, rs, kr, axis=1)
        v_rows = lax.dynamic_slice_in_dim(vg, rs, kr, axis=1)
        kb = jnp.take(k_rows, kcol, axis=2)
        vb = jnp.take(v_rows, kcol, axis=2)
        qb = qr.reshape(b, ncb, NA_COL_BLOCK, h, d)
        sc = jnp.einsum('bnqhd,banchd->bhnqac', qb, kb, preferred_element_type=jnp.float32) * scale
        drow = rs + jnp.arange(kr) - r + row_center
        bias = rpb[:, drow][:, :, dcol_idx].transpose(0, 2, 3, 1, 4)
        sc = sc + bias[None].astype(jnp.float32)
        sc = jnp.where(col_valid[None, None, :, :, None, :], sc, -jnp.inf)
        p = jax.nn.softmax(sc, axis=(-2, -1)).astype(v.dtype)
        o = jnp.einsum('bhnqac,banchd->bnqhd', p, vb)
        return o.reshape(b, GRID_W, h, d)

    out = lax.map(one_row, jnp.arange(rows))
    return out.transpose(1, 0, 2, 3, 4).reshape(b, s, h * d)

def diff_attention(q, k, v, lam_vecs, subln_g, lam_init):
    b, s, _ = q.shape
    q = q.reshape(b, s, DIFF_HEADS, 2, DIFF_HEAD_DIM)
    k = k.reshape(b, s, DIFF_HEADS, 2, DIFF_HEAD_DIM)
    v = v.reshape(b, s, DIFF_HEADS, 2 * DIFF_HEAD_DIM)
    q1, q2 = rope(q[:, :, :, 0], DIFF_ROT_DIM), rope(q[:, :, :, 1], DIFF_ROT_DIM)
    k1, k2 = rope(k[:, :, :, 0], DIFF_ROT_DIM), rope(k[:, :, :, 1], DIFF_ROT_DIM)
    lv = lam_vecs.astype(jnp.float32)
    lam = jnp.exp(jnp.sum(lv[0] * lv[1])) - jnp.exp(jnp.sum(lv[2] * lv[3])) + lam_init
    scale = DIFF_HEAD_DIM ** -0.5
    a1 = blocked_attention(q1, k1, v, scale)
    a2 = blocked_attention(q2, k2, v, scale)
    o = a1 - lam.astype(a1.dtype) * a2
    o = rms_norm(o, subln_g) * (1.0 - lam_init)
    return o.reshape(b, s, DIFF_V_WIDTH)

def latent_attention(c_q, c_kv, k_rope, w_qb, w_kvb, q_norm_g, kv_norm_g):
    b, s, _ = c_q.shape
    q = jnp.einsum('bsr,re->bse', rms_norm(c_q, q_norm_g), w_qb).reshape(b, s, MLA_HEADS, MLA_NOPE_DIM + MLA_ROPE_DIM)
    q = jnp.concatenate([q[..., :MLA_NOPE_DIM], rope(q[..., MLA_NOPE_DIM:], MLA_ROPE_DIM)], -1)
    kv = jnp.einsum('bsr,re->bse', rms_norm(c_kv, kv_norm_g), w_kvb).reshape(b, s, MLA_HEADS, MLA_NOPE_DIM + MLA_V_DIM)
    k_nope, v = kv[..., :MLA_NOPE_DIM], kv[..., MLA_NOPE_DIM:]
    k_r = rope(k_rope[:, :, None, :], MLA_ROPE_DIM)
    k = jnp.concatenate([k_nope, jnp.broadcast_to(k_r, (b, s, MLA_HEADS, MLA_ROPE_DIM))], -1)
    o = blocked_attention(q, k, v, (MLA_NOPE_DIM + MLA_ROPE_DIM) ** -0.5)
    return o.reshape(b, s, MLA_WIDTH)

def first_inputs(seed: int = 0) -> dict:
    key = jax.random.key(seed)
    ks = jax.random.split(key, 20)

    def nrm(k, shape, s):
        return jax.random.normal(k, shape, jnp.float32) * s

    return {
        "x": nrm(ks[0], (BATCH, SEQ, D_MODEL), 1.0),
        "ln_in_g": 1.0 + nrm(ks[1], (D_MODEL,), 0.02),
        "ln_in_b": nrm(ks[2], (D_MODEL,), 0.02),
        "w_in": nrm(ks[3], (DEPTH, D_MODEL, D_IN), D_MODEL ** -0.5),
        "b_gate": nrm(ks[4], (DEPTH, N_BRANCH * D_MODEL), 0.02),
        "na_rpb": nrm(ks[5], (DEPTH, NA_HEADS, 2 * NA_WIN_ROWS - 1, 2 * NA_WIN_COLS - 1), 0.02),
        "diff_lambda": nrm(ks[6], (DEPTH, 4, DIFF_HEAD_DIM), 0.1),
        "diff_subln_g": 1.0 + nrm(ks[7], (DEPTH, 2 * DIFF_HEAD_DIM), 0.02),
        "mla_q_norm_g": 1.0 + nrm(ks[8], (DEPTH, MLA_Q_RANK), 0.02),
        "mla_kv_norm_g": 1.0 + nrm(ks[9], (DEPTH, MLA_KV_RANK), 0.02),
        "w_mla_qb": nrm(ks[10], (DEPTH, MLA_Q_RANK, MLA_HEADS * (MLA_NOPE_DIM + MLA_ROPE_DIM)), MLA_Q_RANK ** -0.5),
        "w_mla_kvb": nrm(ks[11], (DEPTH, MLA_KV_RANK, MLA_HEADS * (MLA_NOPE_DIM + MLA_V_DIM)), MLA_KV_RANK ** -0.5),
        "w_branch": nrm(ks[12], (DEPTH, N_BRANCH, BRANCH_WIDTH, D_MODEL), BRANCH_WIDTH ** -0.5 * DN_BETA),
        "w_out": nrm(ks[13], (DEPTH, D_MODEL, D_MODEL), D_MODEL ** -0.5 * DN_BETA),
        "ln1_g": 1.0 + nrm(ks[14], (DEPTH, D_MODEL), 0.02),
        "ln1_b": nrm(ks[15], (DEPTH, D_MODEL), 0.02),
        "w_ffn_in": nrm(ks[16], (DEPTH, D_MODEL, 2 * D_FF), D_MODEL ** -0.5),
        "w_ffn_out": nrm(ks[17], (DEPTH, D_FF, D_MODEL), D_FF ** -0.5 * DN_BETA),
        "ln2_g": 1.0 + nrm(ks[18], (DEPTH, D_MODEL), 0.02),
        "ln2_b": nrm(ks[19], (DEPTH, D_MODEL), 0.02),
    }

def first_block(x, ln_in_g, ln_in_b, w_in, b_gate, na_rpb, diff_lambda, diff_subln_g,
              mla_q_norm_g, mla_kv_norm_g, w_mla_qb, w_mla_kvb, w_branch, w_out,
              ln1_g, ln1_b, w_ffn_in, w_ffn_out, ln2_g, ln2_b):
    b, s, _ = x.shape
    sizes = (NA_WIDTH, NA_WIDTH, NA_WIDTH, DIFF_QK_WIDTH, DIFF_QK_WIDTH, DIFF_V_WIDTH,
             MLA_Q_RANK, MLA_KV_RANK, MLA_ROPE_DIM, N_BRANCH * D_MODEL)
    split_points = np.cumsum(sizes)[:-1].tolist()

    x = layer_norm(x, ln_in_g, ln_in_b)
    for l in range(DEPTH):
        lam_init = 0.8 - 0.6 * math.exp(-0.3 * l)
        proj = jnp.einsum('bsd,de->bse', x, w_in[l])
        (na_q, na_k, na_v, df_q, df_k, df_v, m_cq, m_ckv, m_kr, gate_pre) = jnp.split(proj, split_points, axis=-1)

        na_out = neighbourhood_attention(
            na_q.reshape(b, s, NA_HEADS, NA_HEAD_DIM), na_k.reshape(b, s, NA_HEADS, NA_HEAD_DIM),
            na_v.reshape(b, s, NA_HEADS, NA_HEAD_DIM), na_rpb[l])
        df_out = diff_attention(df_q, df_k, df_v, diff_lambda[l], diff_subln_g[l], lam_init)
        mla_out = latent_attention(m_cq, m_ckv, m_kr, w_mla_qb[l], w_mla_kvb[l],
                                   mla_q_norm_g[l], mla_kv_norm_g[l])

        gates = jax.nn.sigmoid((gate_pre + b_gate[l]).astype(jnp.float32)).astype(x.dtype)
        gates = gates.reshape(b, s, N_BRANCH, D_MODEL)
        merged = (gates[:, :, 0] * jnp.einsum('bse,ed->bsd', na_out, w_branch[l, 0])
                  + gates[:, :, 1] * jnp.einsum('bse,ed->bsd', df_out, w_branch[l, 1])
                  + gates[:, :, 2] * jnp.einsum('bse,ed->bsd', mla_out, w_branch[l, 2]))
        mix = jnp.einsum('bsd,de->bse', merged, w_out[l])
        x = layer_norm(DN_ALPHA * x + mix, ln1_g[l], ln1_b[l])

        gu = jnp.einsum('bsd,df->bsf', x, w_ffn_in[l])
        hidden = jax.nn.silu(gu[..., :D_FF]) * gu[..., D_FF:]
        ffn = jnp.einsum('bsf,fd->bsd', hidden, w_ffn_out[l])
        x = layer_norm(DN_ALPHA * x + ffn, ln2_g[l], ln2_b[l])
    return x


CHUNK = 128
N_HEADS = 8
N_KV_HEADS = 2
HEAD_DIM = 64
GQA_GROUP = N_HEADS // N_KV_HEADS
ATTN_WIDTH = N_HEADS * HEAD_DIM
KV_WIDTH = N_KV_HEADS * HEAD_DIM
SG_HEADS = 8
SG_HEAD_DIM = 64
SG_WIDTH = SG_HEADS * SG_HEAD_DIM
MIX_WIDTH = ATTN_WIDTH + SG_WIDTH
IN_WIDTH = ATTN_WIDTH + 2 * KV_WIDTH + 2 * SG_WIDTH
D_FF_2 = 2816
CONV_W = 3
ROPE_THETA_2 = 10000.0
EPS = 1e-6


def rms_norm_2(x, g):
    xf = x.astype(jnp.float32)
    y = xf * lax.rsqrt(jnp.mean(xf * xf, axis=-1, keepdims=True) + EPS)
    return (y * g.astype(jnp.float32)).astype(x.dtype)

def axial_rope_tables(seq_len):
    rows = seq_len // GRID_W
    row = jnp.repeat(jnp.arange(rows, dtype=jnp.float32), GRID_W)
    col = jnp.tile(jnp.arange(GRID_W, dtype=jnp.float32), rows)
    axis_dim = HEAD_DIM // 2
    inv_freq = 1.0 / (ROPE_THETA_2 ** (jnp.arange(0, axis_dim, 2, dtype=jnp.float32) / axis_dim))
    ang_r = row[:, None] * inv_freq[None, :]
    ang_c = col[:, None] * inv_freq[None, :]
    return jnp.cos(ang_r), jnp.sin(ang_r), jnp.cos(ang_c), jnp.sin(ang_c)

def rotate(x, cos, sin):
    n = x.shape[-1] // 2
    x1, x2 = x[..., :n], x[..., n:]
    c = cos[None, :, None, :].astype(x.dtype)
    s = sin[None, :, None, :].astype(x.dtype)
    return jnp.concatenate([x1 * c - x2 * s, x2 * c + x1 * s], axis=-1)

def axial_rope(x, tables):
    cr, sr, cc, sc = tables
    half = HEAD_DIM // 2
    return jnp.concatenate([rotate(x[..., :half], cr, sr), rotate(x[..., half:], cc, sc)], axis=-1)

def gqa_attention(q, k, v):
    b, s, _, dh = q.shape
    nblk = s // Q_BLOCK
    qb = q.reshape(b, nblk, Q_BLOCK, N_KV_HEADS, GQA_GROUP, dh)
    qb = jnp.moveaxis(qb, 1, 0)
    scale = HEAD_DIM ** -0.5

    def one_block(qblk):
        sc = jnp.einsum('bqkgd,bskd->bkgqs', qblk, k).astype(jnp.float32) * scale
        p = jax.nn.softmax(sc, axis=-1).astype(v.dtype)
        return jnp.einsum('bkgqs,bskd->bqkgd', p, v)

    o = lax.map(one_block, qb)
    return jnp.moveaxis(o, 0, 1).reshape(b, s, ATTN_WIDTH)

def spatial_gating(u, vv, sg_norm_g, sg_w, sg_b):
    b, s, _ = u.shape
    nc = s // CHUNK
    vv = rms_norm_2(vv.reshape(b, s, SG_HEADS, SG_HEAD_DIM), sg_norm_g)
    vv = vv.reshape(b, nc, CHUNK, SG_HEADS, SG_HEAD_DIM)
    mixed = jnp.einsum('hpq,bnqhd->bnphd', sg_w, vv) + sg_b.T[:, :, None]
    out = u.reshape(b, nc, CHUNK, SG_HEADS, SG_HEAD_DIM) * mixed
    return out.reshape(b, s, SG_WIDTH)

def depthwise_conv(h, w, bias):
    c = h.shape[-1]
    y = lax.conv_general_dilated(h, w[:, None, :].astype(h.dtype), window_strides=(1,),
                                 padding=[(CONV_W // 2, CONV_W // 2)],
                                 dimension_numbers=('NWC', 'WIO', 'NWC'),
                                 feature_group_count=c)
    return y + bias

def second_inputs(seed: int = 0) -> dict:
    key = jax.random.key(seed)
    ks = jax.random.split(key, 17)
    f32 = jnp.float32
    nrm = lambda k, shape, scale: jax.random.normal(k, shape, f32) * scale
    gain = lambda k, shape: 1.0 + 0.05 * jax.random.normal(k, shape, f32)
    return {
        "x": jax.random.normal(ks[0], (BATCH, SEQ, D_MODEL), f32),
        "attn_norm_g": gain(ks[1], (DEPTH, D_MODEL)),
        "w_in": nrm(ks[2], (DEPTH, D_MODEL, IN_WIDTH), D_MODEL ** -0.5),
        "q_norm_g": gain(ks[3], (DEPTH, HEAD_DIM)),
        "k_norm_g": gain(ks[4], (DEPTH, HEAD_DIM)),
        "sg_norm_g": gain(ks[5], (DEPTH, SG_HEADS, SG_HEAD_DIM)),
        "sg_w": nrm(ks[6], (DEPTH, SG_HEADS, CHUNK, CHUNK), 0.5 * CHUNK ** -0.5),
        "sg_b": gain(ks[7], (DEPTH, SG_HEADS, CHUNK)),
        "attn_out_g": gain(ks[8], (DEPTH, ATTN_WIDTH)),
        "sg_out_g": gain(ks[9], (DEPTH, SG_WIDTH)),
        "w_o": nrm(ks[10], (DEPTH, MIX_WIDTH, D_MODEL), MIX_WIDTH ** -0.5),
        "ffn_norm_g": gain(ks[11], (DEPTH, D_MODEL)),
        "w_up": nrm(ks[12], (DEPTH, D_MODEL, 2 * D_FF_2), D_MODEL ** -0.5),
        "conv_w": nrm(ks[13], (DEPTH, CONV_W, 2 * D_FF_2), CONV_W ** -0.5),
        "conv_b": nrm(ks[14], (DEPTH, 2 * D_FF_2), 0.02),
        "w_down": nrm(ks[15], (DEPTH, D_FF_2, D_MODEL), D_FF_2 ** -0.5),
    }

def second_block(x, attn_norm_g, w_in, q_norm_g, k_norm_g, sg_norm_g, sg_w, sg_b,
              attn_out_g, sg_out_g, w_o, ffn_norm_g, w_up, conv_w, conv_b, w_down):
    b, s, _ = x.shape
    tables = axial_rope_tables(s)
    split_at = [ATTN_WIDTH, ATTN_WIDTH + KV_WIDTH, ATTN_WIDTH + 2 * KV_WIDTH,
                ATTN_WIDTH + 2 * KV_WIDTH + SG_WIDTH]
    for i in range(DEPTH):
        h = rms_norm_2(x, attn_norm_g[i])
        proj = h @ w_in[i]
        q, k, v, u, vv = jnp.split(proj, split_at, axis=-1)
        q = rms_norm_2(q.reshape(b, s, N_HEADS, HEAD_DIM), q_norm_g[i])
        k = rms_norm_2(k.reshape(b, s, N_KV_HEADS, HEAD_DIM), k_norm_g[i])
        v = v.reshape(b, s, N_KV_HEADS, HEAD_DIM)
        q = axial_rope(q, tables)
        k = axial_rope(k, tables)
        attn_o = gqa_attention(q, k, v)
        sg_o = spatial_gating(jax.nn.gelu(u), jax.nn.gelu(vv),
                              sg_norm_g[i], sg_w[i], sg_b[i])
        merged = jnp.concatenate([rms_norm_2(attn_o, attn_out_g[i]),
                                  rms_norm_2(sg_o, sg_out_g[i])], axis=-1)
        x = x + merged @ w_o[i]
        h = rms_norm_2(x, ffn_norm_g[i]) @ w_up[i]
        h = depthwise_conv(h, conv_w[i], conv_b[i])
        gate, up = jnp.split(h, 2, axis=-1)
        x = x + (jax.nn.silu(gate) * up) @ w_down[i]
    return x


def setup_inputs(seed=0):
    out = dict(first_inputs(seed))
    for name, value in second_inputs(seed + 1).items():
        if name != "x":
            out[name + "_2"] = value
    return out


def reference(
    x, ln_in_g, ln_in_b, w_in, b_gate, na_rpb, diff_lambda, diff_subln_g, mla_q_norm_g,
    mla_kv_norm_g, w_mla_qb, w_mla_kvb, w_branch, w_out, ln1_g, ln1_b, w_ffn_in, w_ffn_out,
    ln2_g, ln2_b, attn_norm_g_2, w_in_2, q_norm_g_2, k_norm_g_2, sg_norm_g_2, sg_w_2, sg_b_2,
    attn_out_g_2, sg_out_g_2, w_o_2, ffn_norm_g_2, w_up_2, conv_w_2, conv_b_2, w_down_2,
):
    x = first_block(
        x, ln_in_g, ln_in_b, w_in, b_gate, na_rpb, diff_lambda, diff_subln_g, mla_q_norm_g,
        mla_kv_norm_g, w_mla_qb, w_mla_kvb, w_branch, w_out, ln1_g, ln1_b, w_ffn_in, w_ffn_out,
        ln2_g, ln2_b,
    )
    return second_block(
        x, attn_norm_g_2, w_in_2, q_norm_g_2, k_norm_g_2, sg_norm_g_2, sg_w_2, sg_b_2,
        attn_out_g_2, sg_out_g_2, w_o_2, ffn_norm_g_2, w_up_2, conv_w_2, conv_b_2, w_down_2,
    )


_drawn_inputs = setup_inputs


def setup_inputs(seed=0):
    import zlib

    import numpy as np

    out = dict(_drawn_inputs(seed))
    spreads = {}
    factors = {'b_gate': 8.0,
     'na_rpb': 8.0,
     'diff_subln_g': 8.0,
     'mla_q_norm_g': 8.0,
     'mla_kv_norm_g': 8.0,
     'w_mla_qb': 3.157,
     'k_norm_g_2': 2.686,
     'sg_norm_g_2': 3.865,
     'conv_b_2': 3.826}
    for name, (base, spread) in spreads.items():
        noise = np.random.default_rng([zlib.crc32(name.encode()), seed]).standard_normal(out[name].shape)
        drawn = base * np.exp(spread * noise) if base else spread * noise
        out[name] = __import__('jax').numpy.asarray(drawn.astype(out[name].dtype))
    for name, factor in factors.items():
        out[name] = (out[name] * factor).astype(out[name].dtype)
    return out
```

```python
from contextlib import ExitStack
import math

import concourse.bass as bass
from concourse import mybir

F32 = mybir.dt.float32
F32R = mybir.dt.float32r
BF16 = mybir.dt.bfloat16
ALU = mybir.AluOpType
ACT = mybir.ActivationFunctionType
AX = mybir.AxisListType

P = 128
S = 256
D = 1024
DEPTH = 2
RING = 3
PIECE = 2048
FF = 2816
FC = 256
NSTEP = FF // FC
NA_W, DIFF_W = 1536, 1536
MLA_Q, MLA_KV, MLA_R = 384, 256, 32
MLA_COL = NA_W + DIFF_W
PROJ = MLA_COL + MLA_Q + MLA_KV + MLA_R
D_IN = PROJ + 3 * D
IN2 = 1792
ALPHA = (2 * DEPTH) ** 0.25
LN_EPS, RMS_EPS = 1e-5, 1e-6

PER = {
    'w_in1': {'hi': 6, 'lo': 6, 'mm': 6, 'ev': 3, 'n_dma': 6, 'n_split': 6, 'n_mm': 6, 'n_chunk': 3},
    'gates': {'act': 3, 'hi': 6, 'lo': 6, 'mm': 6, 'ev': 3, 'n_dma': 6, 'n_split': 6, 'n_mm': 6, 'n_chunk': 3},
    'ffn0': {'pe': 1, 'act': 2, 'dve': 3, 'hi': 3, 'lo': 3, 'mm': 3, 'n_dma': 3, 'n_split': 3, 'n_mm': 3},
    'layer1': {'pe': 120, 'act': 118, 'dve': 229, 'pool': 10, 'hi': 78, 'lo': 78, 'mm': 78, 'ev': 15, 'par': 35, 'vec': 5, 'n_dma': 78, 'n_split': 78, 'n_mm': 78, 'n_chunk': 15},
    'ffn1': {'pe': 1, 'act': 7, 'dve': 11, 'hi': 3, 'lo': 3, 'mm': 3, 'n_dma': 3, 'n_split': 3, 'n_mm': 3},
    'layer2': {'pe': 56, 'act': 131, 'dve': 214, 'pool': 13, 'hi': 48, 'lo': 48, 'mm': 48, 'ev': 3, 'par': 4, 'n_dma': 48, 'n_split': 48, 'n_mm': 48, 'n_chunk': 3},
}


class Counter:

    def __init__(self, prog, name, sem, unit=1, credit=0):
        self.prog, self.name, self.sem, self.unit = prog, name, sem, unit
        self.counts = [credit]
        prog.counters.append(self)

    def mark(self, instr):
        self.counts[-1] += 1
        if instr is not None:
            instr.then_inc(self.sem, self.unit)
        return self.now()

    def now(self, back=0):
        c = list(self.counts)
        c[-1] -= back
        return (self, tuple(c))

    def static(self):
        return sum(self.counts)


def value(tok, div=1):
    ctr, counts = tok
    v = sum(counts) // div
    for (name, reg), _ in zip(ctr.prog.loops, counts[1:]):
        n = ctr.prog.per.get(name, {}).get(ctr.name, 0) // div
        if n:
            v = reg * n + v
    return v


class Program:

    def __init__(self, nc, per):
        self.nc, self.per, self.loops, self.counters, self.wrong, self.ffns = nc, per, [], [], {}, []

    def loop(self, name, trips):
        prog = self

        class _Loop:
            def __enter__(self):
                self.f = prog.nc.Fori(0, trips)
                reg = self.f.__enter__()
                prog.loops.append((name, reg))
                for c in prog.counters:
                    c.counts.append(0)
                return reg

            def __exit__(self, *a):
                r = self.f.__exit__(*a)
                prog.loops.pop()
                for c in prog.counters:
                    n = c.counts.pop()
                    if n != prog.per.get(name, {}).get(c.name, 0):
                        prog.wrong.setdefault(name, {})[c.name] = n
                    c.counts[-1] += n * trips
                return r
        return _Loop()


def build(nc, t, out, per):
    prog = Program(nc, per)
    with ExitStack() as ctx:
        def sb(name, shape, dt=F32):
            return ctx.enter_context(nc.sbuf_tensor(name, shape, dt))

        def sem(name, unit=1, credit=0):
            s = ctx.enter_context(nc.semaphore(name))
            if credit:
                nc.gpsimd.sem_inc(s, credit)
            return Counter(prog, name, s, unit, credit)

        PE, DV, AC, PO, SP = nc.tensor, nc.vector, nc.scalar, nc.gpsimd, nc.sync

        raw = sb("raw", [P, RING, PIECE])
        whi = sb("whi", [P, RING, PIECE], F32R)
        wlo = sb("wlo", [P, RING, PIECE], F32R)
        x = sb("x", [P, 2, D])
        xTh = sb("xTh", [P, 8, S], F32R)
        xTl = sb("xTl", [P, 8, S], F32R)
        aTh = sb("aTh", [P, 4, S], F32R)
        aTl = sb("aTl", [P, 4, S], F32R)
        proj = sb("proj", [P, 2, PROJ])
        gate = sb("gate", [P, 2, 3 * D])
        vec = sb("vec", [P, 3 * D])
        rpb = sb("rpb", [P, 8, 2, S])
        qk = sb("qk", [P, 2, 2 * S])
        prob = sb("prob", [P, 2, 2, S])
        probT = sb("probT", [P, 2, 2 * S])
        ident = sb("ident", [P, P])
        identb = sb("identb", [P, P], BF16)
        flip8 = sb("flip8", [P, P])
        maskb = sb("maskb", [P, S], BF16)
        rope = sb("rope", [P, 2, 112])
        half = sb("half", [P, 16])
        small = sb("small", [P, 64])
        bn = sb("bn", [P, 2, 2, 6])
        mv = sb("mv", [P, 2, 2])
        rs = sb("rs", [P, 8, 2])
        ri = sb("ri", [P, 8, 2])
        negm = sb("negm", [P, 2, 2, 2])
        pcol = sb("pcol", [P, 32])
        lamc = sb("lamc", [P, 2])
        ps = ctx.enter_context(nc.psum_tensor("ps", [P, 8, 512], F32))

        pe, act, dve, pool = sem("pe"), sem("act"), sem("dve"), sem("pool")
        s_raw = [sem(f"raw{i}", 32) for i in range(RING)]
        s_hi = sem("hi")
        s_lo = sem("lo", credit=RING)
        s_mm = sem("mm", credit=RING)
        s_ev = sem("ev", credit=RING)
        s_par = sem("par", 16)
        s_vec = sem("vec", 16)
        s_out = sem("out", 16)
        s_tick = sem("tick")
        n_dma, n_split, n_mm, n_chunk = (Counter(prog, n, None) for n in ("n_dma", "n_split", "n_mm", "n_chunk"))

        def wait(eng, *toks):
            for k in toks:
                if k is not None:
                    eng.wait_ge(k[0].sem, value(k) * k[0].unit)

        def settle(eng, tok):
            eng.sem_inc(s_tick.sem, 1)

        def fence(eng, *ctrs):
            wait(eng, *(c.now() for c in (*(ctrs or (pe, act, dve, pool)), s_ev) if c.static() > 0 or len(c.counts) > 1))

        def do(eng, ctr, make, *toks):
            wait(eng, *toks)
            return ctr.mark(make())

        def V(make, *toks):
            return do(DV, dve, make, *toks)

        def A(make, *toks):
            return do(AC, act, make, *toks)

        def G(make, *toks):
            wait(PO, *toks)
            if toks:
                settle(PO, toks[0])
            return pool.mark(make())

        def load_piece(src, kts, width, src2=None):
            slot = n_dma.static() % RING
            dst = raw[:, slot, 0:kts * width].rearrange("p (k w) -> p k w", k=kts)
            if src2 is not None:
                parts = [(dst[:, :, 0:width // 2], src), (dst[:, :, width // 2:width], src2)]
            elif kts > 1:
                h = (kts + 1) // 2
                parts = [(dst[:, 0:h], src[:, 0:h]), (dst[:, h:kts], src[:, h:kts])]
            else:
                h = width // 2
                parts = [(dst[:, :, 0:h], src[:, :, 0:h]), (dst[:, :, h:width], src[:, :, h:width])]
            SP.wait_ge(s_lo.sem, value(n_dma.now()) + 1)
            for d, s in parts:
                SP.dma_start(d, s).then_inc(s_raw[slot].sem, 16)
            n_dma.mark(None)

        def split_piece():
            slot = n_split.static() % RING
            n = value(n_split.now())
            AC.wait_ge(s_raw[slot].sem, (value(n_split.now(), RING) + 1) * 32)
            AC.wait_ge(s_mm.sem, n + 1)
            s_hi.mark(AC.activation(whi[:, slot, :], raw[:, slot, :], ACT.Copy))
            DV.wait_ge(s_hi.sem, n + 1)
            s_lo.mark(DV.tensor_tensor(wlo[:, slot, :], raw[:, slot, :], whi[:, slot, :].bitcast(F32),
                                       ALU.subtract))
            n_split.mark(None)

        def open_piece():
            slot = n_mm.static() % RING
            PE.wait_ge(s_lo.sem, value(n_mm.now()) + 1 + RING)
            return slot

        def close_piece(mm):
            s_mm.mark(mm)
            n_mm.mark(None)

        def mul_wide(banks, kt0, kts, width, first, last, th_, tl_, toff=0):
            slot = open_piece()
            h = whi[:, slot, 0:kts * width].rearrange("p (k w) -> p k w", k=kts)
            l = wlo[:, slot, 0:kts * width].rearrange("p (k w) -> p k w", k=kts)
            for k in range(kts):
                for th in range(2):
                    o = ps[:, banks[th], 0:width]
                    ah = th_[:, toff + kt0 + k, th * P:(th + 1) * P]
                    al = tl_[:, toff + kt0 + k, th * P:(th + 1) * P]
                    PE.matmul(o, ah, h[:, k], start=first and k == 0, stop=False)
                    PE.matmul(o, ah, l[:, k], start=False, stop=False)
                    mm = PE.matmul(o, al, h[:, k], start=False, stop=last and k == kts - 1)
            close_piece(mm)

        def mul_narrow(kt0, kts, first, last, th_, tl_, toff=0):
            slot = open_piece()
            h = whi[:, slot, 0:kts * D].rearrange("p (k n w) -> p k n w", k=kts, n=2)
            l = wlo[:, slot, 0:kts * D].rearrange("p (k n w) -> p k n w", k=kts, n=2)
            for k in range(kts):
                for th in range(2):
                    ah = th_[:, toff + kt0 + k, th * P:(th + 1) * P]
                    al = tl_[:, toff + kt0 + k, th * P:(th + 1) * P]
                    o = [ps[:, 4 + 2 * th + n, :] for n in range(2)]
                    for n in range(2):
                        PE.matmul(o[n], ah, h[:, k, n], start=first and k == 0, stop=False)
                    for n in range(2):
                        PE.matmul(o[n], ah, l[:, k, n], start=False, stop=False)
                    for n in range(2):
                        mm = PE.matmul(o[n], al, h[:, k, n], start=False, stop=last and k == kts - 1)
            close_piece(mm)

        def copy_out(dst):
            return lambda o, done, ctr: do(AC, ctr, lambda: AC.activation(dst, o, ACT.Copy), done)

        def chunk(pieces, width, evac, banks=None):
            g = n_chunk.static() % 3
            if banks is None:
                PE.wait_ge(s_ev.sem, value(n_chunk.now()) + 1)
            else:
                g = banks // 2
            kt = 0
            for i, kts in enumerate(pieces):
                mul_wide((2 * g, 2 * g + 1), kt, kts, width, i == 0, i == len(pieces) - 1,
                         xTh, xTl)
                kt += kts
                if i < len(pieces) - 1:
                    split_piece()
            evac(ps[:, 2 * g:2 * g + 2, 0:width], s_mm.now(), s_ev if banks is None else act)
            if banks is None:
                n_chunk.mark(None)
            split_piece()

        def turn(src, nkt, hi, lo, koff=0, bank0=0, widths=None, gain=None, scale=1.0, ready=()):
            fence(PE, act, dve)
            tok = None
            for b in range((nkt + 1) // 2):
                kts = [k for k in (2 * b, 2 * b + 1) if k < nkt]
                bank = ps[:, bank0 + b, :].rearrange("p (k s) -> p k s", k=2)
                wait(PE, *ready)
                for k in kts:
                    for th in range(2):
                        mm = PE.transpose(bank[:, k % 2, th * P:(th + 1) * P], src(k, th), ident[:])
                tt = pe.mark(mm)
                if gain is None:
                    sl = slice(koff + kts[0], koff + kts[-1] + 1)
                    v = bank[:, 0:len(kts), :]
                    th_ = A(lambda: AC.activation(hi[:, sl, :], v, ACT.Copy, scale=scale), tt)
                    tok = V(lambda: DV.scalar_tensor_tensor(out=lo[:, sl, :], in0=v, scalar=scale,
                                                            in1=hi[:, sl, :].bitcast(F32), op0=ALU.mult,
                                                            op1=ALU.subtract), th_)
                else:
                    for k in kts:
                        v, g = bank[:, k % 2, :], gain(k)
                        th_ = A(lambda: AC.activation(hi[:, koff + k, :], v, ACT.Copy, scale=g), tt)
                    for k in kts:
                        v, g = bank[:, k % 2, :], gain(k)
                        tok = V(lambda: DV.scalar_tensor_tensor(out=lo[:, koff + k, :], in0=v, scalar=g,
                                                                in1=hi[:, koff + k, :].bitcast(F32),
                                                                op0=ALU.mult, op1=ALU.subtract), th_)
            wait(PE, tok)
            settle(PE, tok)
            return tok

        def rsqrt(dst, src, mul, eps, *toks):
            n = dst.free_size()
            a = G(lambda: PO.tensor_scalar(dst, src, mul, eps, ALU.mult, ALU.add), *toks)
            hv = half[:, 0:n]
            if len(dst.shape) == 3:
                hv = hv.rearrange("p (a b) -> p a b", a=dst.shape[1])
            return G(lambda: PO.tensor_tensor(dst, dst, hv, ALU.pow), a)

        def layer_norm(gv, bv, *toks):
            tk = None
            for th in range(2):
                for j in range(2):
                    tk = V(lambda: DV.bn_stats(bn[:, th, j, :], x[:, th, j * 512:(j + 1) * 512]), *toks)
            for th in range(2):
                wait(DV, tk)
                settle(DV, tk)
                tb = V(lambda: DV.bn_aggr(mv[:, th, :], bn[:, th, :, :].rearrange("p a b -> p (a b)")))
            r = rsqrt(small[:, 0:2], mv[:, :, 1], 1.0, LN_EPS, tb)
            for th in range(2):
                a = V(lambda: DV.scalar_tensor_tensor(out=x[:, th, :], in0=x[:, th, :], scalar=mv[:, th, 0:1],
                                                      in1=gv, op0=ALU.subtract, op1=ALU.mult), tb)
            for th in range(2):
                a = V(lambda: DV.scalar_tensor_tensor(out=x[:, th, :], in0=x[:, th, :],
                                                      scalar=small[:, th:th + 1], in1=bv, op0=ALU.mult,
                                                      op1=ALU.add), a, r)
            return a

        def x_cols(k, th):
            return x[:, th, k * P:(k + 1) * P]

        def attention(n, pair, qcol, kcol, dk, vcol, dv, scale, out_bank, bias=None, after=None):
            fence(PE, act, dve)
            fence(AC, pe, dve)
            fence(DV, pe, act, pool)
            per_group = 2 if pair else 1
            w = P if pair else dk
            turned, out_of, scored, exped, pturned, pout, mixed = {}, {}, {}, {}, {}, {}, {}

            def turn_qk(g):
                b = ps[0:w, 2 + g % 2, :]
                wait(PE, out_of.get(g - 2))
                settle(PE, dve.now())
                for j, c in enumerate((qcol(g), kcol(g))):
                    for th in range(2):
                        mm = PE.transpose(b[:, j * S + th * P:j * S + (th + 1) * P], proj[:, th, c:c + w],
                                          ident[:])
                turned[g] = pe.mark(mm)
                out_of[g] = V(lambda: DV.tensor_copy(qk[0:w, g % 2, :], b), turned[g])

            def score(h):
                g = h // per_group
                lo_ = 64 * (h % 2) if pair else 0
                kk = 64 if pair else dk
                wait(PE, out_of[g], exped.get(h - 2))
                bank = ps[:, h % 2, :].rearrange("p (t s) -> p t s", t=2)
                for th in range(2):
                    mm = PE.matmul(bank[:, th, :], qk[lo_:lo_ + kk, g % 2, th * P:(th + 1) * P],
                                   qk[lo_:lo_ + kk, g % 2, S:2 * S], start=True, stop=bias is None)
                    if bias is not None:
                        mm = bias(h, th, bank[:, th, :])
                scored[h] = pe.mark(mm)
                m = V(lambda: DV.tensor_reduce(negm[:, h % 2, 0, :], bank, AX.X, ALU.max), scored[h],
                      exped.get(h - 2))
                m = V(lambda: DV.tensor_scalar(negm[:, h % 2, 1, :], negm[:, h % 2, 0, :], -scale, None,
                                               ALU.mult), m)
                wait(AC, m, pturned.get(h - 2))
                for th in range(2):
                    e = AC.activation(prob[:, h % 2, th, :], bank[:, th, :], ACT.Exp,
                                      bias=negm[:, h % 2, 1, th:th + 1], scale=scale,
                                      accum_out=rs[:, h, th:th + 1])
                    exped[h] = act.mark(e)

            def turn_prob(h):
                b = ps[:, 4 + h % 2, :].rearrange("p (k s) -> p k s", k=2)
                wait(PE, exped[h], pout.get(h - 2))
                for kt in range(2):
                    for th in range(2):
                        mm = PE.transpose(b[:, kt, th * P:(th + 1) * P], prob[:, h % 2, th, kt * P:(kt + 1) * P],
                                          ident[:])
                pturned[h] = pe.mark(mm)
                if h % 2:
                    pout[h] = A(lambda: AC.activation(probT[:, h % 2, :], ps[:, 4 + h % 2, :], ACT.Copy), pturned[h])
                else:
                    pout[h] = V(lambda: DV.tensor_copy(probT[:, h % 2, :], ps[:, 4 + h % 2, :]), pturned[h])

            def mix(h):
                wait(PE, pout[h])
                if after is not None:
                    after.before_mix(h)
                for th in range(2):
                    for kt in range(2):
                        mm = PE.matmul(out_bank(h, th), probT[:, h % 2, kt * S + th * P:kt * S + (th + 1) * P],
                                       proj[:, kt, vcol(h):vcol(h) + dv], start=kt == 0, stop=kt == 1)
                mixed[h] = pe.mark(mm)
                if after is not None:
                    after(h, mixed[h])

            turn_qk(0)
            for i in range(n + 2):
                if i < n:
                    score(i)
                    g = i // per_group + 1
                    if i % per_group == 0 and g * per_group < n:
                        turn_qk(g)
                if 1 <= i <= n:
                    turn_prob(i - 1)
                if i >= 2:
                    mix(i - 2)
            return mixed[n - 1]

        def normalise(n, dv, col, done):
            a = V(lambda: DV.reciprocal(ri[:], rs[:]), done)
            for th in range(2):
                wait(DV, a)
                tk = V(lambda: DV.tensor_tensor(
                    proj[:, th, col:col + n * dv].rearrange("p (h d) -> p h d", h=n),
                    ps[:, 6 + th, 0:n * dv].rearrange("p (h d) -> p h d", h=n),
                    ri[:, :, th].unsqueeze(2).broadcast_to([P, n, dv]), ALU.mult))
            return tk

        def rotate(x1, x2, c, s, tmp1, tmp2, shape, *toks):
            V(lambda: DV.tensor_tensor(tmp1, x1, s, ALU.mult), *toks)
            a = V(lambda: DV.tensor_tensor(tmp2, x2, s, ALU.mult), *toks)
            wait(DV, a)
            V(lambda: DV.tensor_tensor(x1, x1, c, ALU.mult))
            b = V(lambda: DV.tensor_tensor(x2, x2, c, ALU.mult))
            wait(DV, b)
            V(lambda: DV.tensor_tensor(x1, x1, tmp2, ALU.subtract))
            return V(lambda: DV.tensor_tensor(x2, x2, tmp1, ALU.add))

        def spread(ap, shape, axis=1):
            return ap.unsqueeze(axis).broadcast_to(shape)

        flipf = gate[:, 0, 0:P]
        wait_c = []
        for dst, src in ((ident[:], t["ident"]), (flip8[:], t["flip8"]), (gate[:, 0, 0:S], t["mask"]),
                         (rope[:], t["rope"].rearrange("(h p) c -> p h c", p=P)),
                         (x[:], t["x"][0].rearrange("(h p) c -> p h c", p=P))):
            s_par.mark(SP.dma_start(dst, src))
        SP.dma_start(vec[:, 0:D], t["ln_g"][0:1, :].broadcast_to([P, D])).then_inc(s_vec.sem, 16)
        SP.dma_start(vec[:, D:2 * D], t["ln_b"][0:1, :].broadcast_to([P, D])).then_inc(s_vec.sem, 16)
        s_vec.counts[-1] += 2
        V(lambda: DV.memset(half[:], -0.5))
        wait(DV, s_par.now())
        V(lambda: DV.tensor_copy(maskb[:], gate[:, 0, 0:S]))
        V(lambda: DV.tensor_copy(identb[:], ident[:]))
        wait(AC, dve.now())
        A(lambda: AC.activation(small[:, 60:61], half[:, 0:1], ACT.Exp))
        wait(PE, dve.now())
        pe.mark(PE.transpose(ps[:, 0, 0:P], ident[:], ident[:]))
        wait(PO, dve.now())
        G(lambda: PO.tensor_copy(small[:, 61:62], half[:, 0:1]))

        def ffn(w_in, w_out, L, first, second, out_banks_read):
            wi = w_in[L].rearrange("(k p) n -> p k n", p=P)
            wo = w_out[L].rearrange("(k p) n -> p k n", p=P)

            def load_up(c):
                for k in (0, 4):
                    load_piece(wi[:, k:k + 4, bass.ds(c * FC, FC)], 4, 2 * FC,
                               wi[:, k:k + 4, bass.ds(c * FC + FF, FC)])

            def up(c, splits):
                mul_wide((0, 1), 0, 4, 2 * FC, True, False, xTh, xTl)
                if splits > 0:
                    split_piece()
                mul_wide((0, 1), 4, 4, 2 * FC, False, True, xTh, xTl)
                first(c, s_mm.now())
                if splits > 1:
                    split_piece()

            def step(c, start, splits=3):
                free, stationary = out_banks_read(), dve.now()
                load_up(c)
                wait(PE, free)
                up(c, splits)
                load_piece(wo[:, bass.ds((c - 1) * 2, 2), :], 2, D)
                wait(PE, stationary)
                mul_narrow(0, 2, start, False, aTh, aTl)
                second(c, split_piece if splits > 2 else (lambda: None))

            fence(PE, act, dve)
            load_up(0)
            up(0, 2)
            second(0, lambda: None)
            step(1, True)
            with prog.loop("ffn%d" % len(prog.ffns), NSTEP - 3) as j:
                step(j + 2, False)
            prog.ffns.append(1)
            step(NSTEP - 1, False, 1)
            load_piece(wo[:, 2 * NSTEP - 2:2 * NSTEP, :], 2, D)
            wait(PE, dve.now())
            mul_narrow(0, 2, False, True, aTh, aTl)

        def narrow_gemm(w, L_pieces, splits):
            wv = w.rearrange("(k p) n -> p k n", p=P)
            kt = 0
            stat = L_pieces[1]
            for i, kts in enumerate(L_pieces[0]):
                load_piece(wv[:, kt:kt + kts, :], kts, D)
                mul_narrow(kt, kts, i == 0, i == len(L_pieces[0]) - 1, *stat)
                kt += kts
                if splits:
                    split_piece()
            return s_mm.now()

        down = ps[:, 4:8, :].rearrange("p (t n) w -> p t (n w)", t=2)
        EIGHT = (2, 2, 1, 1, 1, 1)

        with prog.loop("layer1", DEPTH) as L:
            top = [c.now() for c in (pe, act, dve, pool)]
            for _ in range(RING):
                split_piece()
            w1 = t["w_in"][L].rearrange("(k p) n -> p k n", p=P)

            wait(DV, s_vec.now(), s_par.now(), dve.now())
            a = layer_norm(vec[:, 0:D], vec[:, D:2 * D], dve.now())
            vec_free = a
            turn(x_cols, 8, xTh, xTl, ready=(a,))

            with prog.loop("w_in1", 2) as it:
                for j in range(3):
                    c0 = it * 1536 + j * 512
                    for k in (0, 4):
                        load_piece(w1[:, k:k + 4, bass.ds(c0, 512)], 4, 512)
                    chunk((4, 4), 512, copy_out(proj[:, :, bass.ds(c0, 512)]))
            wait(SP, *top)
            par0 = s_par.now()
            for h in range(8):
                for r in range(4):
                    src = t["rpb"][L, h, 7 - r:11 - r, 0:64]
                    ap = bass.AP(src.tensor, src.offset, [[1, 64], [127, 4], [1, 64]])
                    s_par.mark(SP.dma_start(
                        rpb[64 * (r % 2):64 * (r % 2) + 64, h, r // 2, :].rearrange("p (a c) -> p a c", a=4), ap))
            s_par.mark(SP.dma_start(pcol[:, 0:6], t["pcol1"][L]))
            s_par.mark(SP.dma_start(lamc[:], t["lamc"][bass.ds(L, 1), :].broadcast_to([P, 2])))
            s_par.mark(SP.dma_start(gate[:, 0, 0:256], t["lam"][bass.ds(L, 1), :].broadcast_to([P, 256])))
            wait(SP, vec_free)
            s_vec.mark(SP.dma_start(vec[:, 0:3 * D], t["b_gate"][bass.ds(L, 1), :].broadcast_to([P, 3 * D])))
            for j in range(3):
                c0 = MLA_COL - 0 + j * 224
                for k in (0, 4):
                    load_piece(w1[:, k:k + 4, c0:c0 + 224], 4, 224)
                chunk((4, 4), 224, copy_out(proj[:, :, c0:c0 + 224]))

            lv = gate[:, 0, 0:256].rearrange("p (a b d) -> p a b d", a=2, b=2)
            a = V(lambda: DV.tensor_tensor(gate[:, 1, 0:128].rearrange("p (a d) -> p a d", a=2),
                                           lv[:, :, 0, :], lv[:, :, 1, :], ALU.mult), s_par.now())
            a = V(lambda: DV.tensor_reduce(small[:, 4:6], gate[:, 1, 0:128].rearrange("p (a d) -> p a d", a=2),
                                           AX.X, ALU.add), a)
            a = A(lambda: AC.activation(small[:, 6:8], small[:, 4:6], ACT.Exp), a)
            a = V(lambda: DV.scalar_tensor_tensor(out=small[:, 8:9], in0=small[:, 6:7], scalar=-1.0,
                                                  in1=small[:, 7:8], op0=ALU.mult, op1=ALU.add), a)
            a = V(lambda: DV.tensor_tensor(small[:, 8:9], small[:, 8:9], lamc[:, 0:1], ALU.subtract), a)
            a = V(lambda: DV.tensor_tensor(pcol[:, 6:7], pcol[:, 5:6], lamc[:, 1:2], ALU.mult), a)
            lam_done = a

            with prog.loop("gates", 2) as it:
                for j in range(3):
                    c0 = it * 1536 + j * 512
                    for k in (0, 4):
                        load_piece(w1[:, k:k + 4, bass.ds(c0 + PROJ, 512)], 4, 512)

                    def evac(o, done, ctr):
                        g = gate[:, :, bass.ds(c0, 512)]
                        a = do(DV, ctr, lambda: DV.tensor_tensor(
                            g, o, spread(vec[:, bass.ds(c0, 512)], [P, 2, 512]), ALU.add), done, s_vec.now(), lam_done, s_ev.now())
                        A(lambda: AC.activation(g, g, ACT.Tanh, scale=0.5), a)
                    chunk((4, 4), 512, evac)
            gates_read = s_ev.now()

            def branch(i, src, ready, gain=None):
                turn(src, 4, aTh, aTl, gain=gain, ready=(ready,))
                done = narrow_gemm(t["w_branch"][L, i], ((2, 2), (aTh, aTl)), True)
                g = gate[:, :, i * D:(i + 1) * D]
                wait(DV, done, act.now())
                a = V(lambda: DV.scalar_tensor_tensor(out=g, in0=g, scalar=1.0, in1=down, op0=ALU.add,
                                                      op1=ALU.mult))
                if i:
                    a = V(lambda: DV.tensor_tensor(gate[:, :, 0:D], gate[:, :, 0:D], g, ALU.add), a)
                return a

            def na_bias(h, th, bank):
                PE.matmul(bank, flip8[:], rpb[:, h, th, :], start=False, stop=False)
                return PE.matmul(bank, identb[:], maskb[:], start=False, stop=True)

            wait(PE, s_par.now())
            done = attention(8, True, lambda g: 128 * g, lambda g: 512 + 128 * g, 64,
                             lambda h: 1024 + 64 * h, 64, 0.125,
                             lambda h, th: ps[:, 6 + th, 64 * h:64 * h + 64], bias=na_bias)
            a = normalise(8, 64, 0, done)
            branch(0, lambda k, th: proj[:, th, k * P:(k + 1) * P], a)

            C = NA_W
            rows = proj[:, :, C:C + 1024].rearrange("p t (h d) -> p t h d", d=64)
            tmp = [gate[:, 0, 0:1], None]
            tq = [prob[:].rearrange("p a b s -> p (a b s)")[:, i * S:(i + 1) * S].rearrange(
                "p (t h d) -> p t h d", t=2, h=16) for i in range(2)]
            a = rotate(rows[:, :, :, 0:8], rows[:, :, :, 8:16],
                       spread(rope[:, :, 0:8], [P, 2, 16, 8], 2), spread(rope[:, :, 8:16], [P, 2, 16, 8], 2),
                       tq[0], tq[1], None, act.now(), pe.now(), s_ev.now())
            normed = {}

            class Diff:
                def before_mix(self, h):
                    wait(PE, normed.get(h // 2 - 2))

                def __call__(self, h, done):
                    if h % 2 == 0:
                        return
                    hd = h // 2
                    o = ps[:, 6 + hd % 2, :].rearrange("p (t j d) -> p t j d", t=2, j=2)
                    a = V(lambda: DV.reciprocal(ri[:, 0:2, :], rs[:, h - 1:h + 1, :]), done)
                    b = V(lambda: DV.tensor_scalar(ri[:, 2, :], ri[:, 1, :], small[:, 8:9], None, ALU.mult), a)
                    for th in range(2):
                        y = proj[:, th, C + hd * P:C + (hd + 1) * P]
                        c = V(lambda: DV.tensor_scalar(y, o[:, th, 0, :], ri[:, 0, th:th + 1], None, ALU.mult), b)
                    for th in range(2):
                        y = proj[:, th, C + hd * P:C + (hd + 1) * P]
                        normed[hd] = V(lambda: DV.scalar_tensor_tensor(
                            out=y, in0=o[:, th, 1, :], scalar=ri[:, 2, th:th + 1], in1=y, op0=ALU.mult,
                            op1=ALU.add), c)

            attention(8, True, lambda g: C + 128 * g, lambda g: C + 512 + 128 * g, 64,
                      lambda h: C + 1024 + 128 * (h // 2), 128, 0.125,
                      lambda h, th: ps[:, 6 + (h // 2) % 2, (th * 2 + h % 2) * P:(th * 2 + h % 2 + 1) * P],
                      after=Diff())

            def rms_rows(y, sq, ss, width, *toks):
                a = V(lambda: DV.tensor_tensor(sq, y, y, ALU.mult), *toks)
                return V(lambda: DV.tensor_reduce(ss, sq, AX.X, ALU.add), a)

            y = proj[:, :, C:C + 512].rearrange("p t (h d) -> p t h d", d=P)
            sq = prob[:].rearrange("p a b s -> p (a b s)").rearrange("p (t h d) -> p t h d", t=2, h=4)
            ss = small[:, 16:24].rearrange("p (t h) -> p t h", t=2)
            a = rms_rows(y, sq, ss, P, pe.now(), dve.now())
            r = rsqrt(ss, ss, 1.0 / P, RMS_EPS, a)
            a = V(lambda: DV.tensor_tensor(y, y, ss.unsqueeze(3).broadcast_to([P, 2, 4, P]), ALU.mult), r)
            branch(1, lambda k, th: proj[:, th, C + k * P:C + (k + 1) * P], a, gain=lambda k: pcol[:, 6:7])

            for col, wd, o in ((MLA_COL, MLA_Q, 24), (MLA_COL + MLA_Q, MLA_KV, 26)):
                y = proj[:, :, col:col + wd]
                sq = prob[:].rearrange("p a b s -> p (a b s)")[:, 0:2 * wd].rearrange("p (t d) -> p t d", t=2)
                ss = small[:, o:o + 2]
                a = rms_rows(y, sq, ss, wd, dve.now())
                r = rsqrt(ss, ss, 1.0 / wd, RMS_EPS, a)
                for th in range(2):
                    wait(DV, r)
                    a = V(lambda: DV.tensor_scalar(y[:, th, :], y[:, th, :], small[:, o + th:o + th + 1], None,
                                                   ALU.mult))
            turn(lambda k, th: proj[:, th, MLA_COL + k * P:MLA_COL + (k + 1) * P], 3, xTh, xTl,
                 gain=lambda k: pcol[:, k:k + 1], ready=(a,))
            turn(lambda k, th: proj[:, th, MLA_COL + MLA_Q + k * P:MLA_COL + MLA_Q + (k + 1) * P], 2, xTh, xTl,
                 koff=3, bank0=2, gain=lambda k: pcol[:, 3 + k:4 + k])
            wq = t["w_mla_qb"][L].rearrange("(k p) n -> p k n", p=P)
            fence(PE, act, dve)
            fence(AC, pe, dve)
            for c0, wd in ((0, 512), (512, 256)):
                load_piece(wq[:, :, c0:c0 + wd], 3, wd)
                chunk((3,), wd, copy_out(proj[:, :, c0:c0 + wd]), banks=2 * (c0 > 0))
            load_piece(t["w_mla_kvb"][L].rearrange("(k p) n -> p k n", p=P), 2, D)
            mul_narrow(0, 2, True, True, xTh, xTl, 3)
            split_piece()
            kv = down.rearrange("p t (h e) -> p t h e", e=P)
            kf = proj[:, :, 768:1536].rearrange("p t (h e) -> p t h e", e=96)
            vf = proj[:, :, 1536:2048].rearrange("p t (h e) -> p t h e", e=64)
            wait(AC, s_mm.now())
            for th in range(2):
                A(lambda: AC.activation(kf[:, th, :, 0:64], kv[:, th, :, 0:64], ACT.Copy))
            wait(DV, s_mm.now(), act.now())
            for th in range(2):
                V(lambda: DV.tensor_copy(vf[:, th], kv[:, th, :, 64:128]))
            tq = [prob[:].rearrange("p a b s -> p (a b s)")[:, i * S:(i + 1) * S].rearrange(
                "p (t h d) -> p t h d", t=2, h=8) for i in range(2)]
            qf = proj[:, :, 0:768].rearrange("p t (h e) -> p t h e", e=96)
            cs, sn = rope[:, :, 16:32], rope[:, :, 32:48]
            rotate(qf[:, :, :, 64:80], qf[:, :, :, 80:96], spread(cs, [P, 2, 8, 16], 2),
                   spread(sn, [P, 2, 8, 16], 2), tq[0], tq[1], None)
            kr = proj[:, :, PROJ - MLA_R:PROJ]
            a = rotate(kr[:, :, 0:16], kr[:, :, 16:32], cs, sn, tq[0][:, :, 0, :], tq[1][:, :, 0, :], None,
                       dve.now())
            wait(DV, a)
            for th in range(2):
                V(lambda: DV.tensor_copy(kf[:, th, :, 64:96], spread(kr[:, th, :], [P, 8, 32])))
            done = attention(8, False, lambda h: 96 * h, lambda h: 768 + 96 * h, 96,
                             lambda h: 1536 + 64 * h, 64, 96 ** -0.5,
                             lambda h, th: ps[:, 6 + th, 64 * h:64 * h + 64])
            a = normalise(8, 64, 0, done)
            wait(SP, gates_read)
            s_vec.mark(SP.dma_start(vec[:, 0:D], t["ln1_g"][bass.ds(L, 1), :].broadcast_to([P, D])))
            s_vec.mark(SP.dma_start(vec[:, D:2 * D], t["ln1_b"][bass.ds(L, 1), :].broadcast_to([P, D])))
            ln1_in = s_vec.now()
            a = branch(2, lambda k, th: proj[:, th, k * P:(k + 1) * P], a)

            turn(lambda k, th: gate[:, th, k * P:(k + 1) * P], 8, xTh, xTl, scale=0.5, ready=(a,))
            done = narrow_gemm(t["w_out"][L], (EIGHT, (xTh, xTl)), True)

            def add_down(done, alpha):
                return V(lambda: DV.scalar_tensor_tensor(out=x[:], in0=x[:], scalar=alpha, in1=down,
                                                         op0=ALU.mult, op1=ALU.add), done, pe.now())

            a = add_down(done, ALPHA)
            a = layer_norm(vec[:, 0:D], vec[:, D:2 * D], a, ln1_in)
            ln1_done = a
            turn(x_cols, 8, xTh, xTl, ready=(a,))

            hid = gate[:, :, 0:FC]

            def first1(c, done):
                u = ps[:, 0:2, :]
                a = A(lambda: AC.activation(hid, u[:, :, 0:FC], ACT.Tanh, scale=0.5), done, pe.now())
                a = V(lambda: DV.scalar_tensor_tensor(out=hid, in0=hid, scalar=1.0, in1=u[:, :, 0:FC],
                                                      op0=ALU.add, op1=ALU.mult), a)
                V(lambda: DV.scalar_tensor_tensor(out=hid, in0=hid, scalar=0.5, in1=u[:, :, FC:2 * FC],
                                                  op0=ALU.mult, op1=ALU.mult), a)

            def second1(c, split):
                b = ps[:, 2, :].rearrange("p (k s) -> p k s", k=2)
                wait(PE, dve.now())
                for k in range(2):
                    for th in range(2):
                        mm = PE.transpose(b[:, k, th * P:(th + 1) * P], gate[:, th, k * P:(k + 1) * P], ident[:])
                tt = pe.mark(mm)
                a = A(lambda: AC.activation(aTh[:, 0:2, :], b, ACT.Copy), tt)
                V(lambda: DV.tensor_tensor(aTl[:, 0:2, :], b, aTh[:, 0:2, :].bitcast(F32), ALU.subtract), a)
                split()

            ffn(t["w_ffn_in"], t["w_ffn_out"], L, first1, second1, lambda: dve.now(back=1))
            wait(SP, ln1_done)
            s_vec.mark(SP.dma_start(vec[:, 0:D], t["ln_g"][bass.ds(L + 1, 1), :].broadcast_to([P, D])))
            s_vec.mark(SP.dma_start(vec[:, D:2 * D], t["ln_b"][bass.ds(L + 1, 1), :].broadcast_to([P, D])))
            add_down(s_mm.now(), ALPHA)
        assert (n_mm.static() - RING * 0) % RING == 0 and n_split.static() == n_mm.static() == n_dma.static()

        wait(DV, s_vec.now())
        ln_done = layer_norm(vec[:, 0:D], vec[:, D:2 * D], dve.now())

        scr = gate
        with prog.loop("layer2", DEPTH) as L:
            top = [c.now() for c in (pe, act, dve, pool)]
            for _ in range(RING):
                split_piece()

            def rms_scale(y, dst, width, o, *toks):
                for th in range(2):
                    a = A(lambda: AC.activation(scr[:, th, 2 * D:2 * D + width], y[:, th, :], ACT.Square,
                                                accum_out=small[:, o + th:o + th + 1]), *toks)
                r = rsqrt(small[:, o:o + 2], small[:, o:o + 2], 1.0 / width, RMS_EPS, a)
                wait(DV, r)
                for th in range(2):
                    a = V(lambda: DV.tensor_scalar(dst[:, th, :], y[:, th, :], small[:, o + th:o + th + 1], None,
                                                   ALU.mult))
                return a

            par = []
            SPQ = AC
            wait(SPQ, *top)
            cw = rpb[:].rearrange("p a b c -> p (a b c)")[:, 0:NSTEP * 16].rearrange("p (c f k) -> p c f k", c=NSTEP, f=4)
            sgw = rpb[:].rearrange("p a b c -> p (a b c)")[:, 1024:2048].rearrange("p (h q) -> p h q", h=8)
            for dst, src in ((pcol[:], t["pcol2"][L]), (cw, t["conv"][L]), (sgw, t["sgw"][L]),
                             (vec[:, 0:640], t["brow2"][bass.ds(L, 1), :].broadcast_to([P, 640]))):
                s_par.mark(SPQ.dma_start(dst, src))
            w2 = t["w_in_2"][L].rearrange("(k p) n -> p k n", p=P)
            xn = scr[:, :, 0:D]
            a = rms_scale(x, xn, D, 0, dve.now(), pe.now(), act.now())
            wait(DV, s_par.now())
            wait(AC, s_par.now())
            turn(lambda k, th: scr[:, th, k * P:(k + 1) * P], 8, xTh, xTl, gain=lambda k: pcol[:, k:k + 1],
                 ready=(a,))
            for j in range(4):
                pcs, wd = ((4, 4), 512) if j < 3 else ((3, 3, 2), 256)
                k = 0
                for n in pcs:
                    load_piece(w2[:, k:k + n, j * 512:j * 512 + wd], n, wd)
                    k += n
                chunk(pcs, wd, copy_out(proj[:, :, j * 512:j * 512 + wd]), banks=None if j < 3 else 6)
            y = proj[:, :, 0:640]
            yh = y.rearrange("p t (h d) -> p t h d", d=64)
            sq = scr[:, :, 0:640].rearrange("p t (h d) -> p t h d", d=64)
            ss = small[:, 32:52].rearrange("p (t h) -> p t h", t=2)
            a = V(lambda: DV.tensor_tensor(sq, yh, yh, ALU.mult), act.now(), pe.now(), s_ev.now())
            a = V(lambda: DV.tensor_reduce(ss, sq, AX.X, ALU.add), a)
            hs = half
            a = G(lambda: PO.tensor_scalar(ss, ss, 1.0 / 64, RMS_EPS, ALU.mult, ALU.add), a)
            for th in range(2):
                wait(PO, a)
                settle(PO, a)
                r = G(lambda: PO.tensor_tensor(ss[:, th, :], ss[:, th, :], half[:, 0:10], ALU.pow))
            wait(DV, r)
            for th in range(2):
                a = V(lambda: DV.tensor_tensor(yh[:, th], yh[:, th], ss[:, th, :].unsqueeze(2).broadcast_to([P, 10, 64]),
                                               ALU.mult))
            wait(DV, a)
            for th in range(2):
                a = V(lambda: DV.tensor_tensor(yh[:, th, 0:8], yh[:, th, 0:8], spread(vec[:, 0:64], [P, 8, 64]), ALU.mult))
                a = V(lambda: DV.tensor_tensor(yh[:, th, 8:10], yh[:, th, 8:10], spread(vec[:, 64:128], [P, 2, 64]),
                                               ALU.mult))
            for th in range(2):
                r4 = y[:, th, :].rearrange("p (h a z d) -> p h a z d", a=2, z=2, d=16)
                c4 = rope[:, th, 48:80].rearrange("p (a d) -> p a d", a=2)
                s4 = rope[:, th, 80:112].rearrange("p (a d) -> p a d", a=2)
                tq = [scr[:, th, i * 320:(i + 1) * 320].rearrange("p (h a d) -> p h a d", h=10, a=2) for i in (0, 1)]
                rotate(r4[:, :, :, 0, :], r4[:, :, :, 1, :], spread(c4, [P, 10, 2, 16]), spread(s4, [P, 10, 2, 16]),
                       tq[0], tq[1], None, a)
            done = attention(8, False, lambda h: 64 * h, lambda h: 512 + 64 * (h // 4), 64,
                             lambda h: 640 + 64 * (h // 4), 64, 0.125,
                             lambda h, th: ps[:, 6 + th, 64 * h:64 * h + 64])
            normalise(8, 64, 0, done)

            uv = proj[:, :, 768:1792]
            a = A(lambda: AC.activation(uv, uv, ACT.Gelu_apprx_tanh), act.now(), dve.now())
            v = proj[:, :, 1280:1792]
            vh = v.rearrange("p t (h d) -> p t h d", d=64)
            sq = scr[:, :, 0:512].rearrange("p t (h d) -> p t h d", d=64)
            ss = small[:, 0:16].rearrange("p (t h) -> p t h", t=2)
            a = V(lambda: DV.tensor_tensor(sq, vh, vh, ALU.mult), a, pool.now())
            a = V(lambda: DV.tensor_reduce(ss, sq, AX.X, ALU.add), a)
            r = rsqrt(ss, ss, 1.0 / 64, RMS_EPS, a)
            wait(DV, r)
            for th in range(2):
                a = V(lambda: DV.tensor_tensor(vh[:, th], vh[:, th], ss[:, th, :].unsqueeze(2).broadcast_to([P, 8, 64]),
                                               ALU.mult))
            a = V(lambda: DV.tensor_tensor(v, v, spread(vec[:, 128:640], [P, 2, 512]), ALU.mult), a)
            fence(PE, act, dve)
            for h in range(8):
                mm = PE.matmul(ps[:, h // 4, (h % 4) * P:(h % 4 + 1) * P].rearrange("p (t d) -> p t d", t=2),
                               sgw[:, h, :], vh[:, :, h, :], start=True, stop=True)
            tt = pe.mark(mm)
            mixed = ps[:, 0:2, :].rearrange("p b (h t d) -> p t (b h) d", h=4, t=2)
            wait(DV, tt)
            for th in range(2):
                a = V(lambda: DV.tensor_tensor(vh[:, th], mixed[:, th],
                                               pcol[:, 24:32].unsqueeze(2).broadcast_to([P, 8, 64]), ALU.add))
            a = V(lambda: DV.tensor_tensor(v, v, proj[:, :, 768:1280], ALU.mult), a)
            rms_scale(proj[:, :, 0:512], scr[:, :, 0:512], 512, 24, a)
            a = rms_scale(v, scr[:, :, 512:1024], 512, 26, a, act.now())
            turn(lambda k, th: scr[:, th, k * P:(k + 1) * P], 8, xTh, xTl,
                 gain=lambda k: pcol[:, 16 + k:17 + k], ready=(a,))
            done = narrow_gemm(t["w_o_2"][L], (EIGHT, (xTh, xTl)), True)
            a = V(lambda: DV.tensor_tensor(x[:], x[:], down, ALU.add), done, pe.now())
            a = rms_scale(x, xn, D, 28, a, act.now())
            turn(lambda k, th: scr[:, th, k * P:(k + 1) * P], 8, xTh, xTl,
                 gain=lambda k: pcol[:, 8 + k:9 + k], ready=(a,))

            up4 = scr[:, 0, 0:1024].rearrange("p (t n) -> p t n", t=2)
            conv = scr[:, 0, 1024:2048].rearrange("p (f s) -> p f s", f=4)
            act2 = scr[:, 0, 2048:2560].rearrange("p (f s) -> p f s", f=2)

            def first2(c, done):
                A(lambda: AC.activation(up4, ps[:, 0:2, :], ACT.Copy), done, pe.now())

            def second2(c, split):
                turned = ps[:, 2:4, :].rearrange("p b (f s) -> p (b f) s", f=2)
                wait(PE, act.now(), dve.now())
                for f in range(4):
                    for th in range(2):
                        mm = PE.transpose(turned[:, f, th * P:(th + 1) * P], up4[:, th, f * P:(f + 1) * P], ident[:])
                tt = pe.mark(mm)
                wait(AC, tt, dve.now())
                for f in range(4):
                    w = cw[:, c, f, :] if isinstance(c, int) else cw[:, bass.ds(c, 1), f, :].rearrange("p c k -> p (c k)")
                    a = A(lambda: AC.activation(conv[:, f, :], turned[:, f, :], ACT.Identity, bias=w[:, 3:4],
                                                scale=w[:, 1:2]))
                wait(DV, a)
                for k, dst, src in ((0, slice(1, S), slice(0, S - 1)), (2, slice(0, S - 1), slice(1, S))):
                    for f in range(4):
                        w = cw[:, c, f, :] if isinstance(c, int) else cw[:, bass.ds(c, 1), f, :].rearrange("p c k -> p (c k)")
                        a = V(lambda: DV.scalar_tensor_tensor(out=conv[:, f, dst], in0=turned[:, f, src],
                                                              scalar=w[:, k:k + 1], in1=conv[:, f, dst],
                                                              op0=ALU.mult, op1=ALU.add))
                    wait(DV, a)
                split()
                a = A(lambda: AC.activation(act2, conv[:, 0:2, :], ACT.Tanh, scale=0.5), a)
                a = V(lambda: DV.scalar_tensor_tensor(out=act2, in0=act2, scalar=1.0, in1=conv[:, 0:2, :],
                                                      op0=ALU.add, op1=ALU.mult), a)
                a = V(lambda: DV.scalar_tensor_tensor(out=act2, in0=act2, scalar=0.5, in1=conv[:, 2:4, :],
                                                      op0=ALU.mult, op1=ALU.mult), a)
                a = A(lambda: AC.activation(aTh[:, 0:2, :], act2, ACT.Copy), a, tt)
                V(lambda: DV.tensor_tensor(aTl[:, 0:2, :], act2, aTh[:, 0:2, :].bitcast(F32), ALU.subtract), a)

            ffn(t["w_up_2"], t["w_down_2"], L, first2, second2, lambda: act.now(back=6))
            V(lambda: DV.tensor_tensor(x[:], x[:], down, ALU.add), s_mm.now(), dve.now(), pe.now())

        wait(SP, dve.now())
        s_out.mark(SP.dma_start(out[0].rearrange("(h p) c -> p h c", p=P), x[:]))
        wait(SP, s_out.now())
    return prog.wrong


def constants():
    import numpy as np
    ident = np.eye(P, dtype=np.float32)
    q = np.arange(64)
    flip = np.zeros((P, P), np.float32)
    for b in range(2):
        flip[64 * b + 63 - q, 64 * b + q] = 8.0
    start = np.clip(q - 8, 0, 48)[:, None]
    ok = (q[None, :] >= start) & (q[None, :] < start + 16)
    mask = np.where(np.tile(ok, (2, 4)), 0.0, -1e30).astype(np.float32)
    s = np.arange(S, dtype=np.float32)[:, None]

    def cs(half, theta):
        f = np.exp(-math.log(theta) * np.arange(half, dtype=np.float32) / half).astype(np.float32)
        a = (s * f[None, :]).astype(np.float32)
        return [np.cos(a), np.sin(a)]
    f = (1.0 / (10000.0 ** (np.arange(0, 32, 2, dtype=np.float32) / 32))).astype(np.float32)
    ar, ac = (s // 64) * f, (s % 64) * f
    rope = np.concatenate(cs(8, 500000.0) + cs(16, 500000.0)
                          + [np.cos(ar), np.cos(ac), np.sin(ar), np.sin(ac)], 1).astype(np.float32)
    init = [0.8 - 0.6 * math.exp(-0.3 * l) for l in range(DEPTH)]
    lamc = np.array([[i, 1.0 - i] for i in init], np.float32)
    return {"ident": ident, "flip8": flip, "mask": mask, "rope": rope, "lamc": lamc}


def lay_out(i):
    import numpy as np

    def cols(a):
        return a.reshape(DEPTH, -1, P).transpose(0, 2, 1)
    t = {k: i[k] for k in ("x", "w_in", "b_gate", "w_mla_qb", "w_mla_kvb", "w_branch", "w_out", "ln1_g", "ln1_b",
                           "w_ffn_in", "w_ffn_out", "w_in_2", "w_o_2", "w_up_2", "w_down_2")}
    t["ln_g"] = np.concatenate([i["ln_in_g"][None], i["ln2_g"]], 0)
    t["ln_b"] = np.concatenate([i["ln_in_b"][None], i["ln2_b"]], 0)
    rpb = np.zeros((DEPTH, 8, 15, 127), np.float32)
    rpb[..., 48:79] = i["na_rpb"]
    t["rpb"] = rpb
    t["lam"] = i["diff_lambda"].reshape(DEPTH, 256)
    t["pcol1"] = np.concatenate([cols(i["mla_q_norm_g"]), cols(i["mla_kv_norm_g"]), cols(i["diff_subln_g"])], 2)
    t["pcol2"] = np.concatenate([cols(i["attn_norm_g_2"]), cols(i["ffn_norm_g_2"]), cols(i["attn_out_g_2"]),
                                 cols(i["sg_out_g_2"]), i["sg_b_2"].transpose(0, 2, 1)], 2)
    t["brow2"] = np.concatenate([i["q_norm_g_2"], i["k_norm_g_2"], i["sg_norm_g_2"].reshape(DEPTH, 512)], 1)
    t["sgw"] = i["sg_w_2"].transpose(0, 3, 1, 2)
    cw = np.concatenate([i["conv_w_2"], i["conv_b_2"][:, None]], 1)
    cw = cw.reshape(DEPTH, 4, 2, NSTEP, 2, P)
    t["conv"] = cw.transpose(0, 5, 3, 2, 4, 1).reshape(DEPTH, P, NSTEP, 4, 4)
    t.update(constants())
    return {k: np.ascontiguousarray(v) for k, v in t.items()}


def kernel(**inputs):
    import numpy as np
    import concourse.bacc as bacc
    from concourse.bass_utils import run_bass_kernel_spmd

    arrays = {"in_" + k: v for k, v in lay_out({k: np.asarray(v) for k, v in inputs.items()}).items()}
    nc = bacc.Bacc("TRN2", target_bir_lowering=False, num_devices=1)
    t = {k[3:]: nc.dram_tensor(k, v.shape, F32, kind="ExternalInput").ap() for k, v in arrays.items()}
    out = nc.dram_tensor("out_0", (1, S, D), F32, kind="ExternalOutput").ap()
    wrong = build(nc, t, out, PER)
    assert not wrong, wrong
    r = run_bass_kernel_spmd(nc, [arrays], core_ids=[0])
    return r.results[0]["out_0"]
```

```python
from contextlib import ExitStack
import math

import concourse.bass as bass
from concourse import mybir

F32 = mybir.dt.float32
F32R = mybir.dt.float32r
BF16 = mybir.dt.bfloat16
ALU = mybir.AluOpType
ACT = mybir.ActivationFunctionType
AX = mybir.AxisListType

P = 128
S = 256
D = 1024
DEPTH = 2
RING = 3
PIECE = 2048
FF = 2816
FC = 256
NSTEP = FF // FC
NA_W, DIFF_W = 1536, 1536
MLA_Q, MLA_KV, MLA_R = 384, 256, 32
MLA_COL = NA_W + DIFF_W
GATE0 = 2 * D
PROJ = MLA_COL + MLA_Q + MLA_KV + MLA_R
D_IN = PROJ + 3 * D
IN2 = 1792
ALPHA = (2 * DEPTH) ** 0.25
LN_EPS, RMS_EPS = 1e-5, 1e-6

PER = {
    'w_in1': {'pe': 3, 'hi': 6, 'lo': 6, 'mm': 6, 'ev': 3, 'n_dma': 6, 'n_hi': 6, 'n_split': 6, 'n_mm': 6, 'n_chunk': 3},
    'ffn0': {'pe': 3, 'act': 2, 'dve': 3, 'hi': 3, 'lo': 3, 'mm': 3, 'n_dma': 3, 'n_hi': 3, 'n_split': 3, 'n_mm': 3},
    'layer1': {'pe': 171, 'act': 127, 'dve': 243, 'pool': 14, 'hi': 78, 'lo': 78, 'mm': 78, 'ev': 9, 'vec': 4, 'layer_par': 19, 'b_gate': 1, 'b_gate_last': 1, 'n_dma': 78, 'n_hi': 78, 'n_split': 78, 'n_mm': 78, 'n_chunk': 9},
    'ffn1': {'pe': 3, 'act': 7, 'dve': 11, 'hi': 3, 'lo': 3, 'mm': 3, 'n_dma': 3, 'n_hi': 3, 'n_split': 3, 'n_mm': 3},
    'layer2': {'pe': 85, 'act': 125, 'dve': 210, 'pool': 17, 'hi': 45, 'lo': 45, 'mm': 45, 'par': 4, 'n_dma': 45, 'n_hi': 45, 'n_split': 45, 'n_mm': 45},
}


class Counter:

    def __init__(self, prog, name, sem, unit=1, credit=0):
        self.prog, self.name, self.sem, self.unit = prog, name, sem, unit
        self.counts = [credit]
        prog.counters.append(self)

    def mark(self, instr):
        self.counts[-1] += 1
        if instr is not None:
            instr.then_inc(self.sem, self.unit)
        return self.now()

    def now(self, back=0):
        c = list(self.counts)
        c[-1] -= back
        return (self, tuple(c))

    def static(self):
        return sum(self.counts)


def value(tok, div=1):
    ctr, counts = tok
    v = sum(counts) // div
    for (name, reg), _ in zip(ctr.prog.loops, counts[1:]):
        n = ctr.prog.per.get(name, {}).get(ctr.name, 0) // div
        if n:
            v = reg * n + v
    return v


class Program:

    def __init__(self, nc, per):
        self.nc, self.per, self.loops, self.counters, self.wrong, self.ffns = nc, per, [], [], {}, []

    def loop(self, name, trips):
        prog = self

        class _Loop:
            def __enter__(self):
                self.f = prog.nc.Fori(0, trips)
                reg = self.f.__enter__()
                prog.loops.append((name, reg))
                for c in prog.counters:
                    c.counts.append(0)
                return reg

            def __exit__(self, *a):
                r = self.f.__exit__(*a)
                prog.loops.pop()
                for c in prog.counters:
                    n = c.counts.pop()
                    if n != prog.per.get(name, {}).get(c.name, 0):
                        prog.wrong.setdefault(name, {})[c.name] = n
                    c.counts[-1] += n * trips
                return r
        return _Loop()


def build(nc, t, out, per):
    prog = Program(nc, per)
    with ExitStack() as ctx:
        def sb(name, shape, dt=F32):
            return ctx.enter_context(nc.sbuf_tensor(name, shape, dt))

        def sem(name, unit=1, credit=0):
            s = ctx.enter_context(nc.semaphore(name))
            if credit:
                nc.gpsimd.sem_inc(s, credit)
            return Counter(prog, name, s, unit, credit)

        PE, DV, AC, PO, SP = nc.tensor, nc.vector, nc.scalar, nc.gpsimd, nc.sync

        raw = sb("raw", [P, RING, PIECE])
        whi = sb("whi", [P, RING, PIECE], F32R)
        wlo = sb("wlo", [P, RING, PIECE], F32R)
        x = sb("x", [P, 2, D])
        xTh = sb("xTh", [P, 8, S], F32R)
        xTl = sb("xTl", [P, 8, S], F32R)
        aTh = sb("aTh", [P, 5, S], F32R)
        aTl = sb("aTl", [P, 5, S], F32R)
        proj = sb("proj", [P, 2, PROJ])
        gate = sb("gate", [P, 2, 3 * D])
        vec = sb("vec", [P, 3 * D])
        rpb = sb("rpb", [P, 8, 2, S])
        qk = sb("qk", [P, 2, 2 * S])
        prob = sb("prob", [P, 3, 2, S])
        probT = sb("probT", [P, 2, 2 * S])
        ident = sb("ident", [P, P])
        identb = sb("identb", [P, P], BF16)
        flip8 = sb("flip8", [P, P])
        maskb = sb("maskb", [P, S], BF16)
        rope = sb("rope", [P, 2, 112])
        half = sb("half", [P, 16])
        small = sb("small", [P, 64])
        bn = sb("bn", [P, 2, 2, 6])
        mv = sb("mv", [P, 2, 2])
        rs = sb("rs", [P, 8, 2])
        ri = sb("ri", [P, 8, 2])
        negm = sb("negm", [P, 3, 2, 2])
        pcol = sb("pcol", [P, 32])
        lamc = sb("lamc", [P, 2])
        ps = ctx.enter_context(nc.psum_tensor("ps", [P, 8, 512], F32))

        scratch = prob[:].rearrange("p a b s -> p (a b s)")

        pe, act, dve, pool = sem("pe"), sem("act"), sem("dve"), sem("pool")
        s_raw = [sem(f"raw{i}", 32) for i in range(RING)]
        s_hi = sem("hi")
        s_lo = sem("lo", credit=RING)
        s_mm = sem("mm", credit=RING)
        s_ev = sem("ev", credit=RING)
        s_par = sem("par", 16)
        s_vec = sem("vec", 16)
        s_lay = sem("layer_par", 16)
        s_bg = sem("b_gate", 16)
        s_bg2 = sem("b_gate_last", 16)
        s_out = sem("out", 16)
        s_tick = sem("tick")
        n_dma, n_hi, n_split, n_mm, n_chunk = (Counter(prog, n, None)
                                               for n in ("n_dma", "n_hi", "n_split", "n_mm", "n_chunk"))

        def wait(eng, *toks):
            for k in toks:
                if k is not None:
                    eng.wait_ge(k[0].sem, value(k) * k[0].unit)

        def settle(eng, tok):
            eng.sem_inc(s_tick.sem, 1)

        def fence(eng, *ctrs):
            wait(eng, *(c.now() for c in (*(ctrs or (pe, act, dve, pool)), s_ev) if c.static() > 0 or len(c.counts) > 1))

        def do(eng, ctr, make, *toks):
            wait(eng, *toks)
            return ctr.mark(make())

        def V(make, *toks):
            return do(DV, dve, make, *toks)

        def A(make, *toks):
            return do(AC, act, make, *toks)

        def G(make, *toks):
            wait(PO, *toks)
            if toks:
                settle(PO, toks[0])
            return pool.mark(make())

        def load_piece(src, kts, width, src2=None):
            slot = n_dma.static() % RING
            dst = raw[:, slot, 0:kts * width].rearrange("p (k w) -> p k w", k=kts)
            if src2 is not None:
                parts = [(dst[:, :, 0:width // 2], src), (dst[:, :, width // 2:width], src2)]
            elif kts > 1:
                h = (kts + 1) // 2
                parts = [(dst[:, 0:h], src[:, 0:h]), (dst[:, h:kts], src[:, h:kts])]
            else:
                h = width // 2
                parts = [(dst[:, :, 0:h], src[:, :, 0:h]), (dst[:, :, h:width], src[:, :, h:width])]
            SP.wait_ge(s_lo.sem, value(n_dma.now()) + 1)
            for d, s in parts:
                SP.dma_start(d, s).then_inc(s_raw[slot].sem, 16)
            n_dma.mark(None)

        def split_hi():
            slot = n_hi.static() % RING
            AC.wait_ge(s_raw[slot].sem, (value(n_hi.now(), RING) + 1) * 32)
            AC.wait_ge(s_mm.sem, value(n_hi.now()) + 1)
            s_hi.mark(AC.activation(whi[:, slot, :], raw[:, slot, :], ACT.Copy))
            n_hi.mark(None)

        def split_lo():
            slot = n_split.static() % RING
            DV.wait_ge(s_hi.sem, value(n_split.now()) + 1)
            s_lo.mark(DV.tensor_tensor(wlo[:, slot, :], raw[:, slot, :], whi[:, slot, :].bitcast(F32),
                                       ALU.subtract))
            n_split.mark(None)

        def split_piece():
            split_hi()
            split_lo()

        def multiply(kt0, sizes, outs, width, stat, first=True, last=True, ready=(), toff=0):
            views = []
            for i, kts in enumerate(sizes):
                slot = (n_mm.static() + i) % RING
                n = kts * width * len(outs(0))
                views.append([w[:, slot, 0:n].rearrange("p (k n w) -> p k n w", k=kts, w=width)
                              for w in (whi, wlo)])
            halves = []
            for th in range(2):
                if ready:
                    wait(PE, ready[th]())
                kt = kt0
                for i, kts in enumerate(sizes):
                    h, l = views[i]
                    if th == 0:
                        PE.wait_ge(s_lo.sem, value(n_mm.now()) + 1 + i + RING)
                    for k in range(kts):
                        ah = stat[0][:, toff + kt, th * P:(th + 1) * P]
                        al = stat[1][:, toff + kt, th * P:(th + 1) * P]
                        st = first and kt == kt0
                        sp = last and k == kts - 1 and i == len(sizes) - 1
                        for n, o in enumerate(outs(th)):
                            PE.matmul(o, ah, h[:, k, n], start=st, stop=False)
                        for n, o in enumerate(outs(th)):
                            PE.matmul(o, ah, l[:, k, n], start=False, stop=False)
                        for n, o in enumerate(outs(th)):
                            mm = PE.matmul(o, al, h[:, k, n], start=False, stop=sp)
                        kt += 1
                    if th == 1:
                        s_mm.mark(mm)
                if th == 0:
                    halves.append(pe.mark(mm))
            for _ in sizes:
                n_mm.mark(None)
            return halves + [s_mm.now()]

        def wide(banks, width):
            return lambda th: [ps[:, banks[th], 0:width]]

        def half_bank(bank, width):
            return lambda th: [ps[:, bank, th * width:(th + 1) * width]]

        def narrow(th):
            return [ps[:, 4 + 2 * th + n, :] for n in range(2)]

        def chunk(width, dst):
            g = n_chunk.static() % 3
            PE.wait_ge(s_ev.sem, value(n_chunk.now()) + 1)
            done = multiply(0, (4, 4), wide((2 * g, 2 * g + 1), width), width, (xTh, xTl))
            split_piece()
            do(AC, s_ev, lambda: AC.activation(dst, ps[:, 2 * g:2 * g + 2, 0:width], ACT.Copy), done[1])
            n_chunk.mark(None)
            split_piece()

        def turn_half(src, th, ready, scale=1.0):
            for b in range(2):
                bank = ps[:, 2 * th + b, :].rearrange("p (k s) -> p k s", k=4)
                wait(PE, *ready)
                for k in range(4):
                    mm = PE.transpose(bank[:, k, :], src(4 * b + k, th), ident[:])
                h = xTh[:, 4 * b:4 * b + 4, th * P:(th + 1) * P]
                rounded = A(lambda: AC.activation(h, bank, ACT.Copy, scale=scale), pe.mark(mm))
                tok = V(lambda: DV.scalar_tensor_tensor(
                    out=xTl[:, 4 * b:4 * b + 4, th * P:(th + 1) * P], in0=bank, scalar=scale,
                    in1=h.bitcast(F32), op0=ALU.mult, op1=ALU.subtract), rounded)
            return tok

        def turn(src, nkt, hi, lo, koff=0, bank0=0, gain=None, scale=1.0, ready=(), free=None, hold=True):
            if free is None:
                fence(PE, act, dve)
            else:
                wait(PE, *free)
            tok = None
            for b in range((nkt + 1) // 2):
                kts = [k for k in (2 * b, 2 * b + 1) if k < nkt]
                bank = ps[:, bank0 + b, :].rearrange("p (k s) -> p k s", k=2)
                wait(PE, *ready)
                for k in kts:
                    for th in range(2):
                        mm = PE.transpose(bank[:, k % 2, th * P:(th + 1) * P], src(k, th), ident[:])
                tt = pe.mark(mm)
                if gain is None:
                    sl = slice(koff + kts[0], koff + kts[-1] + 1)
                    v = bank[:, 0:len(kts), :]
                    th_ = A(lambda: AC.activation(hi[:, sl, :], v, ACT.Copy, scale=scale), tt)
                    tok = V(lambda: DV.scalar_tensor_tensor(out=lo[:, sl, :], in0=v, scalar=scale,
                                                            in1=hi[:, sl, :].bitcast(F32), op0=ALU.mult,
                                                            op1=ALU.subtract), th_)
                else:
                    for k in kts:
                        v, g = bank[:, k % 2, :], gain(k)
                        th_ = A(lambda: AC.activation(hi[:, koff + k, :], v, ACT.Copy, scale=g), tt)
                    for k in kts:
                        v, g = bank[:, k % 2, :], gain(k)
                        tok = V(lambda: DV.scalar_tensor_tensor(out=lo[:, koff + k, :], in0=v, scalar=g,
                                                                in1=hi[:, koff + k, :].bitcast(F32),
                                                                op0=ALU.mult, op1=ALU.subtract), th_)
            if hold:
                wait(PE, tok)
                settle(PE, tok)
            return tok

        def rsqrt(dst, src, mul, eps, *toks):
            n = dst.free_size()
            a = G(lambda: PO.tensor_scalar(dst, src, mul, eps, ALU.mult, ALU.add), *toks)
            hv = half[:, 0:n]
            if len(dst.shape) == 3:
                hv = hv.rearrange("p (a b) -> p a b", a=dst.shape[1])
            return G(lambda: PO.tensor_tensor(dst, dst, hv, ALU.pow), a)

        def layer_norm(gv, bv, *toks, add=None, mid=None):
            aggr, r, done = [], [], []
            for th in range(2):
                tk = add(th) if add else None
                for j in range(2):
                    tb = V(lambda: DV.bn_stats(bn[:, th, j, :], x[:, th, j * 512:(j + 1) * 512]), *toks, tk)
                wait(DV, tb)
                settle(DV, tb)
                aggr.append(V(lambda: DV.bn_aggr(mv[:, th, :], bn[:, th, :, :].rearrange("p a b -> p (a b)"))))
                r.append(rsqrt(small[:, th:th + 1], mv[:, th, 1:2], 1.0, LN_EPS, aggr[th]))
            if mid:
                mid()
            for th in range(2):
                a = V(lambda: DV.scalar_tensor_tensor(out=x[:, th, :], in0=x[:, th, :], scalar=mv[:, th, 0:1],
                                                      in1=gv, op0=ALU.subtract, op1=ALU.mult), aggr[th])
                done.append(V(lambda: DV.scalar_tensor_tensor(out=x[:, th, :], in0=x[:, th, :],
                                                              scalar=small[:, th:th + 1], in1=bv, op0=ALU.mult,
                                                              op1=ALU.add), a, r[th]))
            return done

        def x_cols(k, th):
            return x[:, th, k * P:(k + 1) * P]

        def attention(n, pair, qcol, kcol, dk, vcol, dv, scale, out_bank, ready, bias=None, after=None,
                      begin=None, fill=None):
            wait(PE, *ready)
            fence(AC, pe, dve)
            fence(DV, pe, act, pool)
            per_group = 2 if pair else 1
            w = P if pair else dk
            turned, out_of, scored, exped, pturned, pout, mixed = {}, {}, {}, {}, {}, {}, {}

            def turn_qk(g):
                b = ps[0:w, 3, :]
                wait(PE, out_of.get(g - 1))
                settle(PE, dve.now())
                for j, c in enumerate((qcol(g), kcol(g))):
                    for th in range(2):
                        mm = PE.transpose(b[:, j * S + th * P:j * S + (th + 1) * P], proj[:, th, c:c + w],
                                          ident[:])
                turned[g] = pe.mark(mm)
                out_of[g] = V(lambda: DV.tensor_copy(qk[0:w, g % 2, :], b), turned[g])

            def score(h):
                g = h // per_group
                lo_ = 64 * (h % 2) if pair else 0
                kk = 64 if pair else dk
                wait(PE, out_of[g], exped.get(h - 3))
                bank = ps[:, h % 3, :].rearrange("p (t s) -> p t s", t=2)
                for th in range(2):
                    mm = PE.matmul(bank[:, th, :], qk[lo_:lo_ + kk, g % 2, th * P:(th + 1) * P],
                                   qk[lo_:lo_ + kk, g % 2, S:2 * S], start=True, stop=bias is None)
                    if bias is not None:
                        mm = bias(h, th, bank[:, th, :])
                scored[h] = pe.mark(mm)
                m = V(lambda: DV.tensor_reduce(negm[:, h % 3, 0, :], bank, AX.X, ALU.max), scored[h],
                      exped.get(h - 3))
                m = V(lambda: DV.tensor_scalar(negm[:, h % 3, 1, :], negm[:, h % 3, 0, :], -scale, None,
                                               ALU.mult), m)
                wait(AC, m, pturned.get(h - 3))
                for th in range(2):
                    e = AC.activation(prob[:, h % 3, th, :], bank[:, th, :], ACT.Exp,
                                      bias=negm[:, h % 3, 1, th:th + 1], scale=scale,
                                      accum_out=rs[:, h, th:th + 1])
                    exped[h] = act.mark(e)

            def turn_prob(h):
                b = ps[:, 4, :].rearrange("p (k s) -> p k s", k=2)
                wait(PE, exped[h], pout.get(h - 1))
                for kt in range(2):
                    for th in range(2):
                        mm = PE.transpose(b[:, kt, th * P:(th + 1) * P], prob[:, h % 3, th, kt * P:(kt + 1) * P],
                                          ident[:])
                pturned[h] = pe.mark(mm)
                if h % 2:
                    pout[h] = A(lambda: AC.activation(probT[:, h % 2, :], ps[:, 4, :], ACT.Copy), pturned[h])
                else:
                    pout[h] = V(lambda: DV.tensor_copy(probT[:, h % 2, :], ps[:, 4, :]), pturned[h])

            def mix(h):
                wait(PE, pout[h])
                if after is not None:
                    after.before_mix(h)
                for th in range(2):
                    for kt in range(2):
                        mm = PE.matmul(out_bank(h, th), probT[:, h % 2, kt * S + th * P:kt * S + (th + 1) * P],
                                       proj[:, kt, vcol(h):vcol(h) + dv], start=kt == 0, stop=kt == 1)
                mixed[h] = pe.mark(mm)
                if after is not None:
                    after(h, mixed[h])

            turn_qk(0)
            for i in range(n + 3):
                if i < n:
                    g = i // per_group + 1
                    if i % per_group == 0 and g * per_group < n:
                        turn_qk(g)
                    score(i)
                if i == 1 and begin is not None:
                    wait(PE, *begin())
                if fill is not None:
                    fill(i)
                if 2 <= i <= n + 1:
                    turn_prob(i - 2)
                if i >= 3:
                    mix(i - 3)
            return mixed[n - 1]

        def normalise(n, dv, col, done):
            a = V(lambda: DV.reciprocal(ri[:], rs[:]), done)
            for th in range(2):
                wait(DV, a)
                tk = V(lambda: DV.tensor_tensor(
                    proj[:, th, col:col + n * dv].rearrange("p (h d) -> p h d", h=n),
                    ps[:, 6 + th, 0:n * dv].rearrange("p (h d) -> p h d", h=n),
                    ri[:, :, th].unsqueeze(2).broadcast_to([P, n, dv]), ALU.mult))
            return tk

        def rotate(x1, x2, c, s, tmp1, tmp2, shape, *toks):
            V(lambda: DV.tensor_tensor(tmp1, x1, s, ALU.mult), *toks)
            a = V(lambda: DV.tensor_tensor(tmp2, x2, s, ALU.mult), *toks)
            wait(DV, a)
            V(lambda: DV.tensor_tensor(x1, x1, c, ALU.mult))
            b = V(lambda: DV.tensor_tensor(x2, x2, c, ALU.mult))
            wait(DV, b)
            V(lambda: DV.tensor_tensor(x1, x1, tmp2, ALU.subtract))
            return V(lambda: DV.tensor_tensor(x2, x2, tmp1, ALU.add))

        def spread(ap, shape, axis=1):
            return ap.unsqueeze(axis).broadcast_to(shape)

        flipf = gate[:, 0, 0:P]
        wait_c = []
        for dst, src in ((ident[:], t["ident"]), (flip8[:], t["flip8"]), (gate[:, 0, 0:S], t["mask"]),
                         (rope[:], t["rope"].rearrange("(h p) c -> p h c", p=P)),
                         (x[:], t["x"][0].rearrange("(h p) c -> p h c", p=P))):
            s_par.mark(SP.dma_start(dst, src))
        SP.dma_start(vec[:, 0:D], t["ln_g"][0:1, :].broadcast_to([P, D])).then_inc(s_vec.sem, 16)
        SP.dma_start(vec[:, D:2 * D], t["ln_b"][0:1, :].broadcast_to([P, D])).then_inc(s_vec.sem, 16)
        s_vec.counts[-1] += 2
        x_in = s_par.now()
        V(lambda: DV.memset(half[:], -0.5))
        wait(DV, s_par.now())
        V(lambda: DV.tensor_copy(maskb[:], gate[:, 0, 0:S]))
        V(lambda: DV.tensor_copy(identb[:], ident[:]))
        wait(AC, dve.now())
        A(lambda: AC.activation(small[:, 60:61], half[:, 0:1], ACT.Exp))
        wait(PE, dve.now())
        pe.mark(PE.transpose(ps[:, 0, 0:P], ident[:], ident[:]))
        wait(PO, dve.now())
        G(lambda: PO.tensor_copy(small[:, 61:62], half[:, 0:1]))

        def ffn(w_in, w_out, L, first, second, out_banks_read, halves, early=False):
            wi = w_in[L].rearrange("(k p) n -> p k n", p=P)
            wo = w_out[L].rearrange("(k p) n -> p k n", p=P)

            def load_up(c):
                for k in (0, 4):
                    load_piece(wi[:, k:k + 4, bass.ds(c * FC, FC)], 4, 2 * FC,
                               wi[:, k:k + 4, bass.ds(c * FC + FF, FC)])

            def up(c, splits, ready=()):
                done = multiply(0, (4, 4), wide((0, 1), 2 * FC), 2 * FC, (xTh, xTl), ready=ready)
                if splits > 1:
                    split_piece()
                first(c, done[1])
                split_piece()

            def step(c, start, splits=3):
                free, stationary = out_banks_read(), dve.now()
                load_up(c)
                wait(PE, free)
                up(c, splits)
                load_piece(wo[:, bass.ds((c - 1) * 2, 2), :], 2, D)

                def down():
                    wait(PE, stationary)
                    return multiply(0, (2,), narrow, 512, (aTh, aTl), first=start, last=False)[1]

                if splits > 2 or not early:
                    down()
                    second(c, splits > 2, lambda: None)
                else:
                    second(c, False, down)

            load_up(0)
            up(0, 2, halves)
            second(0, False, lambda: None)
            step(1, True)
            with prog.loop("ffn%d" % len(prog.ffns), NSTEP - 3) as j:
                step(j + 2, False)
            prog.ffns.append(1)
            step(NSTEP - 1, False, 1)
            load_piece(wo[:, 2 * NSTEP - 2:2 * NSTEP, :], 2, D)
            wait(PE, dve.now())
            return multiply(0, (2,), narrow, 512, (aTh, aTl), first=False)

        def narrow_gemm(w, groups, stat, late=0, ready=()):
            wv = w.rearrange("(k p) n -> p k n", p=P)
            kt, left = 0, sum(len(g) for g in groups) - late
            for i, sizes in enumerate(groups):
                kt1 = kt
                for kts in sizes:
                    load_piece(wv[:, kt1:kt1 + kts, :], kts, D)
                    kt1 += kts
                done = multiply(kt, sizes, narrow, 512, stat, i == 0, i == len(groups) - 1,
                                ready if i == 0 else ())
                kt = kt1
                for _ in sizes:
                    if left > 0:
                        split_piece()
                    left -= 1
            return done

        down = ps[:, 4:8, :].rearrange("p (t n) w -> p t (n w)", t=2)
        EIGHT = ((2, 2), (1, 1), (1, 1))

        def halves(src, ready, scale=1.0, between=lambda: None):
            def first_half():
                tok = turn_half(src, 0, ready[0], scale)
                between()
                return tok
            return [first_half, lambda: turn_half(src, 1, ready[1], scale)]

        with prog.loop("layer1", DEPTH) as L:
            top = [c.now() for c in (pe, act, dve, pool)]
            for _ in range(RING):
                split_hi()
            w1 = t["w_in"][L].rearrange("(k p) n -> p k n", p=P)
            wait(SP, *top)
            settle(SP, top[0])
            s_bg2.mark(SP.dma_start(vec[:, 2 * D:3 * D], t["b_gate"][bass.ds(L, 1), 2 * D:3 * D].broadcast_to([P, D])))

            wait(DV, s_vec.now(), x_in, dve.now())
            a = layer_norm(vec[:, 0:D], vec[:, D:2 * D], dve.now(), mid=split_lo)
            wait(PO, *top)
            settle(PO, top[0])
            for r in range(4):
                for kr in range(4):
                    src = t["rpb"][L, 0:8, 7 - r + kr, 0:64]
                    ap = bass.AP(src.tensor, src.offset, [[1, 64], [15 * 127, 8], [1, 64]])
                    s_lay.mark(PO.dma_start(rpb[64 * (r % 2):64 * (r % 2) + 64, :, r // 2, kr * 64:(kr + 1) * 64], ap))
            s_lay.mark(PO.dma_start(pcol[:, 0:6], t["pcol1"][L]))
            s_lay.mark(PO.dma_start(lamc[:], t["lamc"][bass.ds(L, 1), :].broadcast_to([P, 2])))
            s_lay.mark(PO.dma_start(gate[:, 0, 0:256], t["lam"][bass.ds(L, 1), :].broadcast_to([P, 256])))
            wait(PO, a[1])
            settle(PO, a[1])
            s_bg.mark(PO.dma_start(vec[:, 0:2 * D], t["b_gate"][bass.ds(L, 1), 0:2 * D].broadcast_to([P, 2 * D])))
            for k in (0, 4):
                load_piece(w1[:, k:k + 4, PROJ + GATE0:PROJ + GATE0 + 512], 4, 512)
            done = multiply(0, (4, 4), wide((6, 7), 512), 512, (xTh, xTl),
                            ready=halves(x_cols, [(a[0],), (a[1],)], between=split_lo))
            split_lo()
            split_piece()
            g = gate[:, :, GATE0:GATE0 + 512]
            a = V(lambda: DV.tensor_tensor(g, ps[:, 6:8, :], spread(vec[:, GATE0:GATE0 + 512], [P, 2, 512]), ALU.add),
                  done[1], s_bg2.now())
            A(lambda: AC.activation(g, g, ACT.Tanh, scale=0.5), a)
            split_piece()

            with prog.loop("w_in1", 2) as it:
                for j in range(3):
                    c0 = it * 1536 + j * 512
                    for k in (0, 4):
                        load_piece(w1[:, k:k + 4, bass.ds(c0, 512)], 4, 512)
                    chunk(512, proj[:, :, bass.ds(c0, 512)])
            wide_out = s_ev.now()

            def latent_chunk(j):
                c0 = MLA_COL + j * 224
                for k in (0, 4):
                    load_piece(w1[:, k:k + 4, c0:c0 + 224], 4, 224)
                chunk(224, proj[:, :, c0:c0 + 224])

            latent_chunk(0)
            C = NA_W
            rows = proj[:, :, C:C + 1024].rearrange("p t (h d) -> p t h d", d=64)
            tq = [scratch[:, i * S:(i + 1) * S].rearrange(
                "p (t h d) -> p t h d", t=2, h=16) for i in range(2)]
            rotate(rows[:, :, :, 0:8], rows[:, :, :, 8:16],
                   spread(rope[:, :, 0:8], [P, 2, 16, 8], 2), spread(rope[:, :, 8:16], [P, 2, 16, 8], 2),
                   tq[0], tq[1], None, dve.now(), wide_out)
            latent_chunk(1)

            lv = gate[:, 0, 0:256].rearrange("p (a b d) -> p a b d", a=2, b=2)
            a = V(lambda: DV.tensor_tensor(gate[:, 1, 0:128].rearrange("p (a d) -> p a d", a=2),
                                           lv[:, :, 0, :], lv[:, :, 1, :], ALU.mult), s_lay.now())
            a = V(lambda: DV.tensor_reduce(small[:, 4:6], gate[:, 1, 0:128].rearrange("p (a d) -> p a d", a=2),
                                           AX.X, ALU.add), a)
            lam_exp = A(lambda: AC.activation(small[:, 6:8], small[:, 4:6], ACT.Exp), a)
            latent_chunk(2)
            a = V(lambda: DV.scalar_tensor_tensor(out=small[:, 8:9], in0=small[:, 6:7], scalar=-1.0,
                                                  in1=small[:, 7:8], op0=ALU.mult, op1=ALU.add), lam_exp)
            a = V(lambda: DV.tensor_tensor(small[:, 8:9], small[:, 8:9], lamc[:, 0:1], ALU.subtract), a)
            a = V(lambda: DV.tensor_tensor(pcol[:, 6:7], pcol[:, 5:6], lamc[:, 1:2], ALU.mult), a)
            lam_done = a

            def gate_pieces():
                for j in range(12):
                    bank, c0 = gate_bank[0], j * 256
                    if GATE0 <= c0 < GATE0 + 512:
                        continue
                    load_piece(w1[:, :, c0 + PROJ:c0 + PROJ + 256], 8, 256)
                    wait(PE, *gate_bank[1])
                    multiply(0, (8,), half_bank(bank, 256), 256, (xTh, xTl))
                    g = gate[:, :, c0:c0 + 256]
                    a = V(lambda: DV.tensor_tensor(g, ps[:, bank, :].rearrange("p (t n) -> p t n", t=2),
                                                   spread(vec[:, c0:c0 + 256], [P, 2, 256]), ALU.add),
                          s_mm.now(), s_bg.now(), lam_done)
                    A(lambda: AC.activation(g, g, ACT.Tanh, scale=0.5), a)
                    gate_bank[1] = gate_read[:] = [a]
                    split_piece()
                    yield

            gate_bank, gate_read = [5, [s_ev.now()]], []
            gates = gate_pieces()

            def fill(*steps):
                return lambda i: next(gates) if i in steps else None

            def branch(i, src, ready, gain=None, free=None, between=None):
                late = 2 if i == 2 else 1
                a = turn(src, 4, aTh, aTl, gain=gain, ready=(ready,), free=free, hold=False)
                if between:
                    between()
                start = (act.now(), dve.now())
                wait(PE, a, *gate_bank[1])
                done = narrow_gemm(t["w_branch"][L, i], ((2, 2),), (aTh, aTl), late=late)

                def merge():
                    wait(DV, act.now())
                    out = []
                    for th in range(2):
                        g = gate[:, th, i * D:(i + 1) * D]
                        a = V(lambda: DV.scalar_tensor_tensor(out=g, in0=g, scalar=1.0, in1=down[:, th], op0=ALU.add,
                                                              op1=ALU.mult), done[th])
                        if i:
                            a = V(lambda: DV.tensor_tensor(gate[:, th, 0:D], gate[:, th, 0:D], g, ALU.add), a)
                        out.append(a)
                    gate_bank[:] = [5, [out[1]]]
                    for _ in range(late):
                        split_piece()
                    return out
                return start, merge

            def begin_with(work):
                def begin():
                    a = work()
                    gate_bank[0] = 2
                    next(gates)
                    gate_bank[0] = 5
                    return [a, *gate_bank[1]]
                return begin

            def na_bias(h, th, bank):
                PE.matmul(bank, flip8[:], rpb[:, h, th, :], start=False, stop=False)
                return PE.matmul(bank, identb[:], maskb[:], start=False, stop=True)

            def rms_rows(y, sq, ss, width, *toks):
                a = V(lambda: DV.tensor_tensor(sq, y, y, ALU.mult), *toks)
                return V(lambda: DV.tensor_reduce(ss, sq, AX.X, ALU.add), a)

            def latent_norms():
                for col, wd, o, free in ((MLA_COL, MLA_Q, 24, D), (MLA_COL + MLA_Q, MLA_KV, 26, D + MLA_Q)):
                    y = proj[:, :, col:col + wd]
                    ss = small[:, o:o + 2]
                    for th in range(2):
                        a = A(lambda: AC.activation(gate[:, th, free:free + wd], y[:, th, :], ACT.Square,
                                                    accum_out=small[:, o + th:o + th + 1]), projected)
                    r = rsqrt(ss, ss, 1.0 / wd, RMS_EPS, a)
                    for th in range(2):
                        wait(DV, r)
                        a = V(lambda: DV.tensor_scalar(y[:, th, :], y[:, th, :], small[:, o + th:o + th + 1], None,
                                                       ALU.mult))
                return a

            projected = s_ev.now()
            wait(PE, s_lay.now())
            done = attention(8, True, lambda g: 128 * g, lambda g: 512 + 128 * g, 64,
                             lambda h: 1024 + 64 * h, 64, 0.125,
                             lambda h, th: ps[:, 6 + th, 64 * h:64 * h + 64], (projected, act.now()),
                             bias=na_bias, begin=begin_with(latent_norms), fill=fill(5, 8))
            a = normalise(8, 64, 0, done)
            free = (act.now(), dve.now())
            start, merge = branch(0, lambda k, th: proj[:, th, k * P:(k + 1) * P], a, free=free,
                                  between=lambda: next(gates))

            normed = {}

            class Diff:
                def before_mix(self, h):
                    wait(PE, normed.get(h // 2 - 2))

                def __call__(self, h, done):
                    if h % 2 == 0:
                        return
                    hd = h // 2
                    o = ps[:, 6 + hd % 2, :].rearrange("p (t j d) -> p t j d", t=2, j=2)
                    a = V(lambda: DV.reciprocal(ri[:, 0:2, :], rs[:, h - 1:h + 1, :]), done)
                    b = V(lambda: DV.tensor_scalar(ri[:, 2, :], ri[:, 1, :], small[:, 8:9], None, ALU.mult), a)
                    for th in range(2):
                        y = proj[:, th, C + hd * P:C + (hd + 1) * P]
                        c = V(lambda: DV.tensor_scalar(y, o[:, th, 0, :], ri[:, 0, th:th + 1], None, ALU.mult), b)
                    for th in range(2):
                        y = proj[:, th, C + hd * P:C + (hd + 1) * P]
                        normed[hd] = V(lambda: DV.scalar_tensor_tensor(
                            out=y, in0=o[:, th, 1, :], scalar=ri[:, 2, th:th + 1], in1=y, op0=ALU.mult,
                            op1=ALU.add), c)

            attention(8, True, lambda g: C + 128 * g, lambda g: C + 512 + 128 * g, 64,
                      lambda h: C + 1024 + 128 * (h // 2), 128, 0.125,
                      lambda h, th: ps[:, 6 + (h // 2) % 2, (th * 2 + h % 2) * P:(th * 2 + h % 2 + 1) * P],
                      start, after=Diff(), begin=begin_with(lambda: merge()[1]), fill=fill(8))

            attn_end = (act.now(), dve.now())
            y = proj[:, :, C:C + 512].rearrange("p t (h d) -> p t h d", d=P)
            sq = scratch[:, 0:1024].rearrange("p (t h d) -> p t h d", t=2, h=4)
            ss = small[:, 16:24].rearrange("p (t h) -> p t h", t=2)
            a = rms_rows(y, sq, ss, P, pe.now(), dve.now())
            r = rsqrt(ss, ss, 1.0 / P, RMS_EPS, a)
            normed_df = V(lambda: DV.tensor_tensor(y, y, ss.unsqueeze(3).broadcast_to([P, 2, 4, P]), ALU.mult), r)

            turn(lambda k, th: proj[:, th, MLA_COL + k * P:MLA_COL + (k + 1) * P], 3, aTh, aTl,
                 gain=lambda k: pcol[:, k:k + 1], free=attn_end, hold=False)
            a = turn(lambda k, th: proj[:, th, MLA_COL + MLA_Q + k * P:MLA_COL + MLA_Q + (k + 1) * P], 2, aTh, aTl,
                     koff=3, bank0=2, gain=lambda k: pcol[:, 3 + k:4 + k], free=attn_end, hold=False)
            next(gates)
            wait(PE, a)
            wq = t["w_mla_qb"][L].rearrange("(k p) n -> p k n", p=P)
            for c0, wd, banks in ((0, 512, (0, 1)), (512, 256, (2, 3))):
                load_piece(wq[:, :, c0:c0 + wd], 3, wd)
                done = multiply(0, (3,), wide(banks, wd), wd, (aTh, aTl))
                A(lambda: AC.activation(proj[:, :, c0:c0 + wd], ps[:, banks[0]:banks[0] + 2, 0:wd], ACT.Copy),
                  done[1])
                split_piece()
            q_out = act.now()
            load_piece(t["w_mla_kvb"][L].rearrange("(k p) n -> p k n", p=P), 2, D)
            wait(PE, *attn_end, *gate_bank[1])
            kv_done = multiply(0, (2,), narrow, 512, (aTh, aTl), toff=3)[1]
            kv = down.rearrange("p t (h e) -> p t h e", e=P)
            kf = proj[:, :, 768:1536].rearrange("p t (h e) -> p t h e", e=96)
            vf = proj[:, :, 1536:2048].rearrange("p t (h e) -> p t h e", e=64)
            for th in range(2):
                k_out = A(lambda: AC.activation(kf[:, th, :, 0:64], kv[:, th, :, 0:64], ACT.Copy), kv_done)
            split_piece()

            def latent_rest():
                for th in range(2):
                    v_out = V(lambda: DV.tensor_copy(vf[:, th], kv[:, th, :, 64:128]), kv_done, k_out, pe.now())
                gate_bank[:] = [2, [q_out]]
                next(gates)
                gate_bank[1] = [*gate_bank[1], v_out, k_out]
                tq = [scratch[:, i * S:(i + 1) * S].rearrange(
                    "p (t h d) -> p t h d", t=2, h=8) for i in range(2)]
                qf = proj[:, :, 0:768].rearrange("p t (h e) -> p t h e", e=96)
                cs, sn = rope[:, :, 16:32], rope[:, :, 32:48]
                rotate(qf[:, :, :, 64:80], qf[:, :, :, 80:96], spread(cs, [P, 2, 8, 16], 2),
                       spread(sn, [P, 2, 8, 16], 2), tq[0], tq[1], None, q_out)
                kr = proj[:, :, PROJ - MLA_R:PROJ]
                a = rotate(kr[:, :, 0:16], kr[:, :, 16:32], cs, sn, tq[0][:, :, 0, :], tq[1][:, :, 0, :], None,
                           dve.now())
                wait(DV, a)
                for th in range(2):
                    V(lambda: DV.tensor_copy(kf[:, th, :, 64:96], spread(kr[:, th, :], [P, 8, 32])))

            start, merge = branch(1, lambda k, th: proj[:, th, C + k * P:C + (k + 1) * P], normed_df,
                                  gain=lambda k: pcol[:, 6:7], free=(q_out,), between=latent_rest)
            done = attention(8, False, lambda h: 96 * h, lambda h: 768 + 96 * h, 96,
                             lambda h: 1536 + 64 * h, 64, 96 ** -0.5,
                             lambda h, th: ps[:, 6 + th, 64 * h:64 * h + 64], start,
                             begin=begin_with(lambda: merge()[1]))
            a = normalise(8, 64, 0, done)
            _, merge = branch(2, lambda k, th: proj[:, th, k * P:(k + 1) * P], a,
                              between=lambda: next(gates))
            a = merge()
            assert next(gates, 0) == 0
            wait(SP, *gate_read)
            s_vec.mark(SP.dma_start(vec[:, 0:D], t["ln1_g"][bass.ds(L, 1), :].broadcast_to([P, D])))
            s_vec.mark(SP.dma_start(vec[:, D:2 * D], t["ln1_b"][bass.ds(L, 1), :].broadcast_to([P, D])))
            ln1_in = s_vec.now()

            done = narrow_gemm(t["w_out"][L], EIGHT, (xTh, xTl), late=2,
                               ready=halves(lambda k, th: gate[:, th, k * P:(k + 1) * P], [(a[0],), (a[1],)], 0.5))

            def add_down(done, alpha, th):
                return V(lambda: DV.scalar_tensor_tensor(out=x[:, th], in0=x[:, th], scalar=alpha, in1=down[:, th],
                                                         op0=ALU.mult, op1=ALU.add), done, pe.now())

            a = layer_norm(vec[:, 0:D], vec[:, D:2 * D], ln1_in, add=lambda th: add_down(done[th], ALPHA, th))
            ln1_done = a[1]

            def two_splits():
                split_piece()
                split_piece()

            hid = gate[:, :, 0:FC]

            def first1(c, done):
                u = ps[:, 0:2, :]
                a = A(lambda: AC.activation(hid, u[:, :, 0:FC], ACT.Tanh, scale=0.5), done, pe.now())
                a = V(lambda: DV.scalar_tensor_tensor(out=hid, in0=hid, scalar=1.0, in1=u[:, :, 0:FC],
                                                      op0=ALU.add, op1=ALU.mult), a)
                V(lambda: DV.scalar_tensor_tensor(out=hid, in0=hid, scalar=0.5, in1=u[:, :, FC:2 * FC],
                                                  op0=ALU.mult, op1=ALU.mult), a)

            def second1(c, split, middle):
                b = ps[:, 2, :].rearrange("p (k s) -> p k s", k=2)
                wait(PE, dve.now())
                for k in range(2):
                    for th in range(2):
                        mm = PE.transpose(b[:, k, th * P:(th + 1) * P], gate[:, th, k * P:(k + 1) * P], ident[:])
                tt = pe.mark(mm)
                a = A(lambda: AC.activation(aTh[:, 0:2, :], b, ACT.Copy), tt)
                V(lambda: DV.tensor_tensor(aTl[:, 0:2, :], b, aTh[:, 0:2, :].bitcast(F32), ALU.subtract), a)
                if split:
                    split_piece()

            done = ffn(t["w_ffn_in"], t["w_ffn_out"], L, first1, second1, lambda: dve.now(back=1),
                       halves(x_cols, [(a[0],), (a[1],)], between=two_splits))
            wait(SP, ln1_done)
            s_vec.mark(SP.dma_start(vec[:, 0:D], t["ln_g"][bass.ds(L + 1, 1), :].broadcast_to([P, D])))
            s_vec.mark(SP.dma_start(vec[:, D:2 * D], t["ln_b"][bass.ds(L + 1, 1), :].broadcast_to([P, D])))
            for th in range(2):
                add_down(done[th], ALPHA, th)
        assert (n_mm.static() - RING * 0) % RING == 0 and n_split.static() == n_mm.static() == n_dma.static()

        wait(DV, s_vec.now())
        ln_done = layer_norm(vec[:, 0:D], vec[:, D:2 * D], dve.now())

        scr = gate
        with prog.loop("layer2", DEPTH) as L:
            top = [c.now() for c in (pe, act, dve, pool)]
            x_done = (dve.now(back=1), dve.now())
            for _ in range(RING):
                split_hi()

            def halves2(src, ready, between):
                return halves(src, [(r,) for r in ready], between=between)

            def rms_scale(y, dst, width, o, *toks, mid=None):
                for th in range(2):
                    a = A(lambda: AC.activation(scr[:, th, 2 * D:2 * D + width], y[:, th, :], ACT.Square,
                                                accum_out=small[:, o + th:o + th + 1]), *toks)
                r = rsqrt(small[:, o:o + 2], small[:, o:o + 2], 1.0 / width, RMS_EPS, a)
                if mid:
                    mid()
                wait(DV, r)
                for th in range(2):
                    a = V(lambda: DV.tensor_scalar(dst[:, th, :], y[:, th, :], small[:, o + th:o + th + 1], None,
                                                   ALU.mult))
                return a

            par = []
            SPQ = AC
            wait(SPQ, *top)
            cw = rpb[:].rearrange("p a b c -> p (a b c)")[:, 0:NSTEP * 16].rearrange("p (c f k) -> p c f k", c=NSTEP, f=4)
            sgw = rpb[:].rearrange("p a b c -> p (a b c)")[:, 1024:2048].rearrange("p (h q) -> p h q", h=8)
            for dst, src in ((pcol[:], t["pcol2"][L]), (cw, t["conv"][L]), (sgw, t["sgw"][L]),
                             (vec[:, 0:640 + 2 * D], t["brow2"][bass.ds(L, 1), :].broadcast_to([P, 640 + 2 * D]))):
                s_par.mark(SPQ.dma_start(dst, src))
            w2 = t["w_in_2"][L].rearrange("(k p) n -> p k n", p=P)
            def rms_x(col, o, *toks, mid=lambda: None):
                r = []
                for th in range(2):
                    a = A(lambda: AC.activation(scr[:, th, 2 * D:3 * D], x[:, th, :], ACT.Square,
                                                accum_out=small[:, o + th:o + th + 1]), toks[th])
                    r.append(rsqrt(small[:, o + th:o + th + 1], small[:, o + th:o + th + 1], 1.0 / D, RMS_EPS, a))
                mid()
                return [V(lambda: DV.scalar_tensor_tensor(out=scr[:, th, 0:D], in0=x[:, th, :],
                                                          scalar=small[:, o + th:o + th + 1],
                                                          in1=vec[:, col:col + D], op0=ALU.mult, op1=ALU.mult),
                          r[th], s_par.now()) for th in range(2)]

            def scr_cols(k, th):
                return scr[:, th, k * P:(k + 1) * P]

            before = (pe.now(), act.now())
            wait(AC, *before)
            a = rms_x(640, 0, x_done[0], x_done[1], mid=split_lo)
            wait(DV, s_par.now())
            wait(AC, s_par.now())

            def project(c0, wd, banks, func=ACT.Copy, between=lambda: None, ready=(), late=lambda: None):
                for k in (0, 4):
                    load_piece(w2[:, k:k + 4, c0:c0 + wd], 4, wd)
                done = multiply(0, (4, 4), wide(banks, wd), wd, (xTh, xTl), ready=ready)
                late()
                split_piece()
                between()
                A(lambda: AC.activation(proj[:, :, c0:c0 + wd], ps[:, banks[0]:banks[0] + 2, 0:wd], func), done[1])
                split_piece()
                between()

            project(0, 512, (4, 5), ready=halves2(scr_cols, a, split_lo), late=split_lo)
            project(512, 256, (6, 7))

            y = proj[:, :, 0:640]
            yh = y.rearrange("p t (h d) -> p t h d", d=64)
            sq = scr[:, :, 0:640].rearrange("p t (h d) -> p t h d", d=64)
            ssq = small[:, 32:52].rearrange("p (t h) -> p t h", t=2)

            def norm_qk():
                a = V(lambda: DV.tensor_tensor(sq, yh, yh, ALU.mult), qkv_out, xt_done)
                a = V(lambda: DV.tensor_reduce(ssq, sq, AX.X, ALU.add), a)
                a = G(lambda: PO.tensor_scalar(ssq, ssq, 1.0 / 64, RMS_EPS, ALU.mult, ALU.add), a)
                for th in range(2):
                    wait(PO, a)
                    settle(PO, a)
                    r = G(lambda: PO.tensor_tensor(ssq[:, th, :], ssq[:, th, :], half[:, 0:10], ALU.pow))
                yield
                wait(DV, r)
                for th in range(2):
                    a = V(lambda: DV.tensor_tensor(yh[:, th], yh[:, th],
                                                   ssq[:, th, :].unsqueeze(2).broadcast_to([P, 10, 64]), ALU.mult))
                wait(DV, a)
                for th in range(2):
                    a = V(lambda: DV.tensor_tensor(yh[:, th, 0:8], yh[:, th, 0:8], spread(vec[:, 0:64], [P, 8, 64]),
                                                   ALU.mult))
                    a = V(lambda: DV.tensor_tensor(yh[:, th, 8:10], yh[:, th, 8:10],
                                                   spread(vec[:, 64:128], [P, 2, 64]), ALU.mult))
                yield
                for th in range(2):
                    r4 = y[:, th, :].rearrange("p (h a z d) -> p h a z d", a=2, z=2, d=16)
                    c4 = rope[:, th, 48:80].rearrange("p (a d) -> p a d", a=2)
                    s4 = rope[:, th, 80:112].rearrange("p (a d) -> p a d", a=2)
                    tq = [scr[:, th, i * 320:(i + 1) * 320].rearrange("p (h a d) -> p h a d", h=10, a=2)
                          for i in (0, 1)]
                    rotate(r4[:, :, :, 0, :], r4[:, :, :, 1, :], spread(c4, [P, 10, 2, 16]),
                           spread(s4, [P, 10, 2, 16]), tq[0], tq[1], None, a)
                    yield

            qkv_out, xt_done = act.now(), pe.now()
            norm = norm_qk()
            next(norm)
            project(768, 512, (0, 1), ACT.Gelu_apprx_tanh, lambda: next(norm))
            project(1280, 512, (2, 3), ACT.Gelu_apprx_tanh, lambda: next(norm, None))
            uv_out = act.now()

            u, v = proj[:, :, 768:1280], proj[:, :, 1280:1792]
            vh = v.rearrange("p t (h d) -> p t h d", d=64)
            sv = scr[:, :, 1280:1792].rearrange("p t (h d) -> p t h d", d=64)
            ssv = small[:, 0:16].rearrange("p (t h) -> p t h", t=2)

            def gating():
                a = V(lambda: DV.tensor_tensor(sv, vh, vh, ALU.mult), uv_out, pool.now())
                a = V(lambda: DV.tensor_reduce(ssv, sv, AX.X, ALU.add), a)
                r = rsqrt(ssv, ssv, 1.0 / 64, RMS_EPS, a)
                yield
                yield
                for th in range(2):
                    a = V(lambda: DV.tensor_tensor(vh[:, th], vh[:, th],
                                                   ssv[:, th, :].unsqueeze(2).broadcast_to([P, 8, 64]), ALU.mult), r)
                vn = V(lambda: DV.tensor_tensor(v, v, spread(vec[:, 128:640], [P, 2, 512]), ALU.mult), a)
                a = None
                for g in range(2):
                    wait(PE, vn, a)
                    for h in range(4 * g, 4 * g + 4):
                        mm = PE.matmul(ps[:, 5, (h % 4) * P:(h % 4 + 1) * P].rearrange("p (t d) -> p t d", t=2),
                                       sgw[:, h, :], vh[:, :, h, :], start=True, stop=True)
                    tt = pe.mark(mm)
                    yield
                    mixed = ps[:, 5, :].rearrange("p (h t d) -> p t h d", h=4, t=2)
                    for th in range(2):
                        a = V(lambda: DV.tensor_tensor(
                            vh[:, th, 4 * g:4 * g + 4], mixed[:, th],
                            pcol[:, 24 + 4 * g:28 + 4 * g].unsqueeze(2).broadcast_to([P, 4, 64]), ALU.add), tt)
                a = V(lambda: DV.tensor_tensor(v, v, u, ALU.mult), a)
                yield
                rms_scale(v, scr[:, :, 512:1024], 512, 26, a, act.now())
                yield

            gate_steps = gating()
            done = attention(8, False, lambda h: 64 * h, lambda h: 512 + 64 * (h // 4), 64,
                             lambda h: 640 + 64 * (h // 4), 64, 0.125,
                             lambda h, th: ps[:, 6 + th, 64 * h:64 * h + 64], (act.now(), dve.now()),
                             fill=lambda i: next(gate_steps, None) if i else None)
            sg_done = dve.now()
            assert next(gate_steps, 0) == 0
            a = normalise(8, 64, 0, done)
            free = (act.now(), a)
            a = rms_scale(proj[:, :, 0:512], scr[:, :, 0:512], 512, 24, a, act.now())
            turn(lambda k, th: scr[:, th, (4 + k) * P:(5 + k) * P], 4, xTh, xTl, koff=4, bank0=2,
                 gain=lambda k: pcol[:, 20 + k:21 + k], ready=(sg_done,), free=free, hold=False)
            turn(lambda k, th: scr[:, th, k * P:(k + 1) * P], 4, xTh, xTl,
                 gain=lambda k: pcol[:, 16 + k:17 + k], ready=(a,), free=free)
            done = narrow_gemm(t["w_o_2"][L], ((2, 2), (2, 2)), (xTh, xTl), late=2)
            a = [V(lambda: DV.tensor_tensor(x[:, th], x[:, th], down[:, th], ALU.add), done[th]) for th in range(2)]
            a = rms_x(640 + D, 28, *a)

            def two_splits():
                split_piece()
                split_piece()

            up4 = scr[:, 0, 0:1024].rearrange("p (t n) -> p t n", t=2)
            conv = scr[:, 0, 1024:2048].rearrange("p (f s) -> p f s", f=4)
            act2 = scr[:, 0, 2048:2560].rearrange("p (f s) -> p f s", f=2)

            def first2(c, done):
                A(lambda: AC.activation(up4, ps[:, 0:2, :], ACT.Copy), done, pe.now())

            def second2(c, split, middle):
                turned = ps[:, 2:4, :].rearrange("p b (f s) -> p (b f) s", f=2)
                wait(PE, act.now(), dve.now())
                for f in range(4):
                    for th in range(2):
                        mm = PE.transpose(turned[:, f, th * P:(th + 1) * P], up4[:, th, f * P:(f + 1) * P], ident[:])
                tt = pe.mark(mm)
                middle()
                if split:
                    split_piece()
                product = s_mm.now()
                wait(AC, tt, dve.now())
                for f in range(4):
                    w = cw[:, c, f, :] if isinstance(c, int) else cw[:, bass.ds(c, 1), f, :].rearrange("p c k -> p (c k)")
                    a = A(lambda: AC.activation(conv[:, f, :], turned[:, f, :], ACT.Identity, bias=w[:, 3:4],
                                                scale=w[:, 1:2]))
                wait(DV, a)
                for k, dst, src in ((0, slice(1, S), slice(0, S - 1)), (2, slice(0, S - 1), slice(1, S))):
                    for f in range(4):
                        w = cw[:, c, f, :] if isinstance(c, int) else cw[:, bass.ds(c, 1), f, :].rearrange("p c k -> p (c k)")
                        a = V(lambda: DV.scalar_tensor_tensor(out=conv[:, f, dst], in0=turned[:, f, src],
                                                              scalar=w[:, k:k + 1], in1=conv[:, f, dst],
                                                              op0=ALU.mult, op1=ALU.add))
                    wait(DV, a)
                a = A(lambda: AC.activation(act2, conv[:, 0:2, :], ACT.Tanh, scale=0.5), a)
                a = V(lambda: DV.scalar_tensor_tensor(out=act2, in0=act2, scalar=1.0, in1=conv[:, 0:2, :],
                                                      op0=ALU.add, op1=ALU.mult), a)
                a = V(lambda: DV.scalar_tensor_tensor(out=act2, in0=act2, scalar=0.5, in1=conv[:, 2:4, :],
                                                      op0=ALU.mult, op1=ALU.mult), a)
                a = A(lambda: AC.activation(aTh[:, 0:2, :], act2, ACT.Copy), a, product)
                V(lambda: DV.tensor_tensor(aTl[:, 0:2, :], act2, aTh[:, 0:2, :].bitcast(F32), ALU.subtract), a)

            done = ffn(t["w_up_2"], t["w_down_2"], L, first2, second2, lambda: act.now(back=6),
                       halves2(scr_cols, a, two_splits), early=True)
            for th in range(2):
                V(lambda: DV.tensor_tensor(x[:, th], x[:, th], down[:, th], ALU.add), done[th], dve.now(back=th))

        wait(SP, dve.now())
        s_out.mark(SP.dma_start(out[0].rearrange("(h p) c -> p h c", p=P), x[:]))
        wait(SP, s_out.now())
    return prog.wrong


def constants():
    import numpy as np
    ident = np.eye(P, dtype=np.float32)
    q = np.arange(64)
    flip = np.zeros((P, P), np.float32)
    for b in range(2):
        flip[64 * b + 63 - q, 64 * b + q] = 8.0
    start = np.clip(q - 8, 0, 48)[:, None]
    ok = (q[None, :] >= start) & (q[None, :] < start + 16)
    mask = np.where(np.tile(ok, (2, 4)), 0.0, -1e30).astype(np.float32)
    s = np.arange(S, dtype=np.float32)[:, None]

    def cs(half, theta):
        f = np.exp(-math.log(theta) * np.arange(half, dtype=np.float32) / half).astype(np.float32)
        a = (s * f[None, :]).astype(np.float32)
        return [np.cos(a), np.sin(a)]
    f = (1.0 / (10000.0 ** (np.arange(0, 32, 2, dtype=np.float32) / 32))).astype(np.float32)
    ar, ac = (s // 64) * f, (s % 64) * f
    rope = np.concatenate(cs(8, 500000.0) + cs(16, 500000.0)
                          + [np.cos(ar), np.cos(ac), np.sin(ar), np.sin(ac)], 1).astype(np.float32)
    init = [0.8 - 0.6 * math.exp(-0.3 * l) for l in range(DEPTH)]
    lamc = np.array([[i, 1.0 - i] for i in init], np.float32)
    return {"ident": ident, "flip8": flip, "mask": mask, "rope": rope, "lamc": lamc}


def lay_out(i):
    import numpy as np

    def cols(a):
        return a.reshape(DEPTH, -1, P).transpose(0, 2, 1)
    t = {k: i[k] for k in ("x", "w_in", "b_gate", "w_mla_qb", "w_mla_kvb", "w_branch", "w_out", "ln1_g", "ln1_b",
                           "w_ffn_in", "w_ffn_out", "w_in_2", "w_o_2", "w_up_2", "w_down_2")}
    t["ln_g"] = np.concatenate([i["ln_in_g"][None], i["ln2_g"]], 0)
    t["ln_b"] = np.concatenate([i["ln_in_b"][None], i["ln2_b"]], 0)
    rpb = np.zeros((DEPTH, 8, 15, 127), np.float32)
    rpb[..., 48:79] = i["na_rpb"]
    t["rpb"] = rpb
    t["lam"] = i["diff_lambda"].reshape(DEPTH, 256)
    t["pcol1"] = np.concatenate([cols(i["mla_q_norm_g"]), cols(i["mla_kv_norm_g"]), cols(i["diff_subln_g"])], 2)
    t["pcol2"] = np.concatenate([cols(i["attn_norm_g_2"]), cols(i["ffn_norm_g_2"]), cols(i["attn_out_g_2"]),
                                 cols(i["sg_out_g_2"]), i["sg_b_2"].transpose(0, 2, 1)], 2)
    t["brow2"] = np.concatenate([i["q_norm_g_2"], i["k_norm_g_2"], i["sg_norm_g_2"].reshape(DEPTH, 512),
                                 i["attn_norm_g_2"], i["ffn_norm_g_2"]], 1)
    t["sgw"] = i["sg_w_2"].transpose(0, 3, 1, 2)
    cw = np.concatenate([i["conv_w_2"], i["conv_b_2"][:, None]], 1)
    cw = cw.reshape(DEPTH, 4, 2, NSTEP, 2, P)
    t["conv"] = cw.transpose(0, 5, 3, 2, 4, 1).reshape(DEPTH, P, NSTEP, 4, 4)
    t.update(constants())
    return {k: np.ascontiguousarray(v) for k, v in t.items()}


def kernel(**inputs):
    import numpy as np
    import concourse.bacc as bacc
    from concourse.bass_utils import run_bass_kernel_spmd

    arrays = {"in_" + k: v for k, v in lay_out({k: np.asarray(v) for k, v in inputs.items()}).items()}
    nc = bacc.Bacc("TRN2", target_bir_lowering=False, num_devices=1)
    t = {k[3:]: nc.dram_tensor(k, v.shape, F32, kind="ExternalInput").ap() for k, v in arrays.items()}
    out = nc.dram_tensor("out_0", (1, S, D), F32, kind="ExternalOutput").ap()
    wrong = build(nc, t, out, PER)
    assert not wrong, wrong
    r = run_bass_kernel_spmd(nc, [arrays], core_ids=[0])
    return r.results[0]["out_0"]
```

```python
from contextlib import ExitStack
import math

import concourse.bass as bass
from concourse import mybir

F32 = mybir.dt.float32
F32R = mybir.dt.float32r
BF16 = mybir.dt.bfloat16
ALU = mybir.AluOpType
ACT = mybir.ActivationFunctionType
AX = mybir.AxisListType

P = 128
S = 256
D = 1024
DEPTH = 2
RING = 3
PIECE = 2048
FF = 2816
FC = 256
NSTEP = FF // FC
NA_W, DIFF_W = 1536, 1536
MLA_Q, MLA_KV, MLA_R = 384, 256, 32
MLA_COL = NA_W + DIFF_W
GATE0 = 2 * D
PROJ = MLA_COL + MLA_Q + MLA_KV + MLA_R
D_IN = PROJ + 3 * D
IN2 = 1792
ALPHA = (2 * DEPTH) ** 0.25
LN_EPS, RMS_EPS = 1e-5, 1e-6

PER = {
    'w_in1': {'pe': 3, 'hi': 6, 'lo': 6, 'mm': 6, 'ev': 3, 'n_dma': 6, 'n_hi': 6, 'n_split': 6, 'n_mm': 6, 'n_chunk': 3},
    'ffn0': {'pe': 3, 'act': 2, 'dve': 3, 'hi': 3, 'lo': 3, 'mm': 3, 'n_dma': 3, 'n_hi': 3, 'n_split': 3, 'n_mm': 3},
    'layer1': {'pe': 171, 'act': 139, 'dve': 229, 'pool': 16, 'hi': 78, 'lo': 78, 'mm': 78, 'ev': 9, 'vec': 4, 'layer_par': 19, 'b_gate': 1, 'b_gate_last': 1, 'n_dma': 78, 'n_hi': 78, 'n_split': 78, 'n_mm': 78, 'n_chunk': 9},
    'ffn1': {'pe': 3, 'act': 7, 'dve': 11, 'hi': 3, 'lo': 3, 'mm': 3, 'n_dma': 3, 'n_hi': 3, 'n_split': 3, 'n_mm': 3},
    'layer2': {'pe': 85, 'act': 129, 'dve': 206, 'pool': 17, 'hi': 45, 'lo': 45, 'mm': 45, 'par': 5, 'n_dma': 45, 'n_hi': 45, 'n_split': 45, 'n_mm': 45},
}


class Counter:

    def __init__(self, prog, name, sem, unit=1, credit=0):
        self.prog, self.name, self.sem, self.unit = prog, name, sem, unit
        self.counts = [credit]
        prog.counters.append(self)

    def mark(self, instr):
        self.counts[-1] += 1
        if instr is not None:
            instr.then_inc(self.sem, self.unit)
        return self.now()

    def now(self, back=0):
        c = list(self.counts)
        c[-1] -= back
        return (self, tuple(c))

    def static(self):
        return sum(self.counts)


def value(tok, div=1):
    ctr, counts = tok
    v = sum(counts) // div
    for (name, reg), _ in zip(ctr.prog.loops, counts[1:]):
        n = ctr.prog.per.get(name, {}).get(ctr.name, 0) // div
        if n:
            v = reg * n + v
    return v


class Program:

    def __init__(self, nc, per):
        self.nc, self.per, self.loops, self.counters, self.wrong, self.ffns = nc, per, [], [], {}, []

    def loop(self, name, trips):
        prog = self

        class _Loop:
            def __enter__(self):
                self.f = prog.nc.Fori(0, trips)
                reg = self.f.__enter__()
                prog.loops.append((name, reg))
                for c in prog.counters:
                    c.counts.append(0)
                return reg

            def __exit__(self, *a):
                r = self.f.__exit__(*a)
                prog.loops.pop()
                for c in prog.counters:
                    n = c.counts.pop()
                    if n != prog.per.get(name, {}).get(c.name, 0):
                        prog.wrong.setdefault(name, {})[c.name] = n
                    c.counts[-1] += n * trips
                return r
        return _Loop()


def build(nc, t, out, per):
    prog = Program(nc, per)
    with ExitStack() as ctx:
        def sb(name, shape, dt=F32):
            return ctx.enter_context(nc.sbuf_tensor(name, shape, dt))

        def sem(name, unit=1, credit=0):
            s = ctx.enter_context(nc.semaphore(name))
            if credit:
                nc.gpsimd.sem_inc(s, credit)
            return Counter(prog, name, s, unit, credit)

        PE, DV, AC, PO, SP = nc.tensor, nc.vector, nc.scalar, nc.gpsimd, nc.sync

        raw = sb("raw", [P, RING, PIECE])
        whi = sb("whi", [P, RING, PIECE], F32R)
        wlo = sb("wlo", [P, RING, PIECE], F32R)
        x = sb("x", [P, 2, D])
        xTh = sb("xTh", [P, 8, S], F32R)
        xTl = sb("xTl", [P, 8, S], F32R)
        aTh = sb("aTh", [P, 5, S], F32R)
        aTl = sb("aTl", [P, 5, S], F32R)
        proj = sb("proj", [P, 2, PROJ])
        gate = sb("gate", [P, 2, 3 * D])
        vec = sb("vec", [P, 3 * D])
        rpb = sb("rpb", [P, 8, 2, S])
        qk = sb("qk", [P, 2, 2 * S])
        prob = sb("prob", [P, 3, 2, S])
        probT = sb("probT", [P, 2, 2 * S])
        ident = sb("ident", [P, P])
        identb = sb("identb", [P, P], BF16)
        flip8 = sb("flip8", [P, P])
        maskb = sb("maskb", [P, S], BF16)
        rope = sb("rope", [P, 2, 112])
        half = sb("half", [P, 16])
        small = sb("small", [P, 64])
        bn = sb("bn", [P, 2, 2, 6])
        mv = sb("mv", [P, 2, 2])
        rs = sb("rs", [P, 8, 2])
        ri = sb("ri", [P, 8, 2])
        negm = sb("negm", [P, 3, 2, 2])
        pcol = sb("pcol", [P, 32])
        lamc = sb("lamc", [P, 2])
        ps = ctx.enter_context(nc.psum_tensor("ps", [P, 8, 512], F32))

        scratch = prob[:].rearrange("p a b s -> p (a b s)")

        pe, act, dve, pool = sem("pe"), sem("act"), sem("dve"), sem("pool")
        s_raw = [sem(f"raw{i}", 32) for i in range(RING)]
        s_hi = sem("hi")
        s_lo = sem("lo", credit=RING)
        s_mm = sem("mm", credit=RING)
        s_ev = sem("ev", credit=RING)
        s_x = sem("x_in", 16)
        s_par = sem("par", 16)
        s_vec = sem("vec", 16)
        s_lay = sem("layer_par", 16)
        s_bg = sem("b_gate", 16)
        s_bg2 = sem("b_gate_last", 16)
        s_out = sem("out", 16)
        s_tick = sem("tick")
        n_dma, n_hi, n_split, n_mm, n_chunk = (Counter(prog, n, None)
                                               for n in ("n_dma", "n_hi", "n_split", "n_mm", "n_chunk"))

        def wait(eng, *toks):
            latest = {}
            for k in toks:
                if k is not None:
                    key = (k[0].name, len(k[1]))
                    latest[key] = max(latest.get(key, k), k, key=lambda t: sum(t[1]))
            for k in latest.values():
                eng.wait_ge(k[0].sem, value(k) * k[0].unit)

        def settle(eng):
            eng.sem_inc(s_tick.sem, 1)

        def fence(eng, *ctrs):
            wait(eng, *(c.now() for c in (*(ctrs or (pe, act, dve, pool)), s_ev) if c.static() > 0 or len(c.counts) > 1))

        def do(eng, ctr, make, *toks):
            wait(eng, *toks)
            return ctr.mark(make())

        def V(make, *toks):
            return do(DV, dve, make, *toks)

        def A(make, *toks):
            return do(AC, act, make, *toks)

        def G(make, *toks):
            wait(PO, *toks)
            if toks:
                settle(PO)
            return pool.mark(make())

        def load_piece(src, kts, width, src2=None):
            slot = n_dma.static() % RING
            dst = raw[:, slot, 0:kts * width].rearrange("p (k w) -> p k w", k=kts)
            if src2 is not None:
                parts = [(dst[:, :, 0:width // 2], src), (dst[:, :, width // 2:width], src2)]
            elif kts > 1:
                h = (kts + 1) // 2
                parts = [(dst[:, 0:h], src[:, 0:h]), (dst[:, h:kts], src[:, h:kts])]
            else:
                h = width // 2
                parts = [(dst[:, :, 0:h], src[:, :, 0:h]), (dst[:, :, h:width], src[:, :, h:width])]
            SP.wait_ge(s_lo.sem, value(n_dma.now()) + 1)
            for d, s in parts:
                SP.dma_start(d, s).then_inc(s_raw[slot].sem, 16)
            n_dma.mark(None)

        def split_hi(cols=PIECE):
            slot = n_hi.static() % RING
            AC.wait_ge(s_raw[slot].sem, (value(n_hi.now(), RING) + 1) * 32)
            AC.wait_ge(s_mm.sem, value(n_hi.now()) + 1)
            s_hi.mark(AC.activation(whi[:, slot, 0:cols], raw[:, slot, 0:cols], ACT.Copy))
            n_hi.mark(None)

        def split_lo(cols=PIECE):
            slot = n_split.static() % RING
            DV.wait_ge(s_hi.sem, value(n_split.now()) + 1)
            s_lo.mark(DV.tensor_tensor(wlo[:, slot, 0:cols], raw[:, slot, 0:cols],
                                       whi[:, slot, 0:cols].bitcast(F32),
                                       ALU.subtract))
            n_split.mark(None)

        behind = [RING]

        def catch_up(keep=0, cols=PIECE):
            while behind[0] > keep:
                split_hi(cols)
                split_lo(cols)
                behind[0] -= 1

        def split_one():
            catch_up(max(behind[0] - 1, 0))

        def multiply(kt0, sizes, outs, width, stat, first=True, last=True, ready=(), toff=0, keep=0):
            if not ready:
                catch_up(keep)
            views = []
            for i, kts in enumerate(sizes):
                slot = (n_mm.static() + i) % RING
                n = kts * width * len(outs(0))
                views.append([w[:, slot, 0:n].rearrange("p (k n w) -> p k n w", k=kts, w=width)
                              for w in (whi, wlo)])
            halves, there = [], [None, None]
            if ready:
                there[0] = ready[0]()
            for th in range(2):
                wait(PE, there[th])
                kt = kt0
                for i, kts in enumerate(sizes):
                    h, l = views[i]
                    if th == 0:
                        PE.wait_ge(s_lo.sem, value(n_mm.now()) + 1 + i + RING)
                    for k in range(kts):
                        ah = stat[0][:, toff + kt, th * P:(th + 1) * P]
                        al = stat[1][:, toff + kt, th * P:(th + 1) * P]
                        st = first and kt == kt0
                        sp = last and k == kts - 1 and i == len(sizes) - 1
                        for n, o in enumerate(outs(th)):
                            PE.matmul(o, ah, h[:, k, n], start=st, stop=False)
                        for n, o in enumerate(outs(th)):
                            PE.matmul(o, ah, l[:, k, n], start=False, stop=False)
                        for n, o in enumerate(outs(th)):
                            mm = PE.matmul(o, al, h[:, k, n], start=False, stop=sp)
                        kt += 1
                        if ready and th == 0 and 4 * (kt - kt0) == 3 * sum(sizes):
                            there[1] = ready[1]()
                    if th == 1:
                        s_mm.mark(mm)
                if th == 0:
                    halves.append(pe.mark(mm))
            for _ in sizes:
                n_mm.mark(None)
                behind[0] += 1
            return halves + [s_mm.now()]

        def wide(banks, width):
            return lambda th: [ps[:, banks[th], 0:width]]

        def half_bank(bank, width):
            return lambda th: [ps[:, bank, th * width:(th + 1) * width]]

        def narrow(th):
            return [ps[:, 4 + 2 * th + n, :] for n in range(2)]

        def chunk(width, dst, keep=0, cols=(PIECE, PIECE)):
            g = n_chunk.static() % 3
            PE.wait_ge(s_ev.sem, value(n_chunk.now()) + 1)
            done = multiply(0, (4, 4), wide((2 * g, 2 * g + 1), width), width, (xTh, xTl))
            catch_up(1, cols[0])
            do(AC, s_ev, lambda: AC.activation(dst, ps[:, 2 * g:2 * g + 2, 0:width], ACT.Copy), done[1])
            n_chunk.mark(None)
            catch_up(keep, cols[1])

        def turn_half(src, th, ready, scale=1.0):
            for b in range(2):
                bank = ps[:, 2 * th + b, :].rearrange("p (k s) -> p k s", k=4)
                wait(PE, *ready)
                for k in range(4):
                    mm = PE.transpose(bank[:, k, :], src(4 * b + k, th), ident[:])
                h = xTh[:, 4 * b:4 * b + 4, th * P:(th + 1) * P]
                rounded = A(lambda: AC.activation(h, bank, ACT.Copy, scale=scale), pe.mark(mm))
                tok = V(lambda: DV.scalar_tensor_tensor(
                    out=xTl[:, 4 * b:4 * b + 4, th * P:(th + 1) * P], in0=bank, scalar=scale,
                    in1=h.bitcast(F32), op0=ALU.mult, op1=ALU.subtract), rounded)
            return tok

        def turn(src, nkt, hi, lo, koff=0, bank0=0, gain=None, scale=1.0, ready=(), free=None, hold=True):
            if free is None:
                fence(PE, act, dve)
            else:
                wait(PE, *free)
            tok = None
            for b in range((nkt + 1) // 2):
                kts = [k for k in (2 * b, 2 * b + 1) if k < nkt]
                bank = ps[:, bank0 + b, :].rearrange("p (k s) -> p k s", k=2)
                wait(PE, *ready)
                for k in kts:
                    for th in range(2):
                        mm = PE.transpose(bank[:, k % 2, th * P:(th + 1) * P], src(k, th), ident[:])
                tt = pe.mark(mm)
                if gain is None:
                    sl = slice(koff + kts[0], koff + kts[-1] + 1)
                    v = bank[:, 0:len(kts), :]
                    th_ = A(lambda: AC.activation(hi[:, sl, :], v, ACT.Copy, scale=scale), tt)
                    tok = V(lambda: DV.scalar_tensor_tensor(out=lo[:, sl, :], in0=v, scalar=scale,
                                                            in1=hi[:, sl, :].bitcast(F32), op0=ALU.mult,
                                                            op1=ALU.subtract), th_)
                else:
                    for k in kts:
                        v, g = bank[:, k % 2, :], gain(k)
                        th_ = A(lambda: AC.activation(hi[:, koff + k, :], v, ACT.Copy, scale=g), tt)
                    for k in kts:
                        v, g = bank[:, k % 2, :], gain(k)
                        tok = V(lambda: DV.scalar_tensor_tensor(out=lo[:, koff + k, :], in0=v, scalar=g,
                                                                in1=hi[:, koff + k, :].bitcast(F32),
                                                                op0=ALU.mult, op1=ALU.subtract), th_)
            if hold:
                wait(PE, tok)
                settle(PE)
            return tok

        def rsqrt(dst, src, mul, eps, *toks):
            n = dst.free_size()
            a = G(lambda: PO.tensor_scalar(dst, src, mul, eps, ALU.mult, ALU.add), *toks)
            hv = half[:, 0:n]
            if len(dst.shape) == 3:
                hv = hv.rearrange("p (a b) -> p a b", a=dst.shape[1])
            return G(lambda: PO.tensor_tensor(dst, dst, hv, ALU.pow), a)

        def norm_stats(th, *toks):
            for j in range(2):
                tb = V(lambda: DV.bn_stats(bn[:, th, j, :], x[:, th, j * 512:(j + 1) * 512]), *toks)
            wait(DV, tb)
            settle(DV)
            a = V(lambda: DV.bn_aggr(mv[:, th, :], bn[:, th, :, :].rearrange("p a b -> p (a b)")))
            return rsqrt(small[:, th:th + 1], mv[:, th, 1:2], 1.0, LN_EPS, a)

        def norm_apply(th, *toks):
            a = V(lambda: DV.scalar_tensor_tensor(out=x[:, th, :], in0=x[:, th, :], scalar=mv[:, th, 0:1],
                                                  in1=vec[:, 0:D], op0=ALU.subtract, op1=ALU.mult), *toks)
            return V(lambda: DV.scalar_tensor_tensor(out=x[:, th, :], in0=x[:, th, :],
                                                     scalar=small[:, th:th + 1], in1=vec[:, D:2 * D],
                                                     op0=ALU.mult, op1=ALU.add), a)

        def x_cols(k, th):
            return x[:, th, k * P:(k + 1) * P]

        def attention(n, pair, qcol, kcol, dk, vcol, dv, scale, out_bank, ready, bias=None, after=None,
                      begin=None, fill=None):
            wait(PE, *ready)
            fence(AC, pe, dve)
            fence(DV, pe, act, pool)
            per_group = 2 if pair else 1
            w = P if pair else dk
            turned, out_of, scored, exped, pturned, pout, mixed = {}, {}, {}, {}, {}, {}, {}

            def turn_qk(g):
                b = ps[0:w, 3, :]
                wait(PE, out_of.get(g - 1))
                settle(PE)
                for j, c in enumerate((qcol(g), kcol(g))):
                    for th in range(2):
                        mm = PE.transpose(b[:, j * S + th * P:j * S + (th + 1) * P], proj[:, th, c:c + w],
                                          ident[:])
                turned[g] = pe.mark(mm)
                out_of[g] = V(lambda: DV.tensor_copy(qk[0:w, g % 2, :], b), turned[g])

            def score(h):
                g = h // per_group
                lo_ = 64 * (h % 2) if pair else 0
                kk = 64 if pair else dk
                wait(PE, out_of[g], exped.get(h - 3))
                bank = ps[:, h % 3, :].rearrange("p (t s) -> p t s", t=2)
                for th in range(2):
                    mm = PE.matmul(bank[:, th, :], qk[lo_:lo_ + kk, g % 2, th * P:(th + 1) * P],
                                   qk[lo_:lo_ + kk, g % 2, S:2 * S], start=True, stop=bias is None)
                    if bias is not None:
                        mm = bias(h, th, bank[:, th, :])
                scored[h] = pe.mark(mm)
                m = V(lambda: DV.tensor_reduce(negm[:, h % 3, 0, :], bank, AX.X, ALU.max), scored[h],
                      exped.get(h - 3))
                m = V(lambda: DV.tensor_scalar(negm[:, h % 3, 1, :], negm[:, h % 3, 0, :], -scale, None,
                                               ALU.mult), m)
                wait(AC, m, pturned.get(h - 3))
                for th in range(2):
                    e = AC.activation(prob[:, h % 3, th, :], bank[:, th, :], ACT.Exp,
                                      bias=negm[:, h % 3, 1, th:th + 1], scale=scale,
                                      accum_out=rs[:, h, th:th + 1])
                    exped[h] = act.mark(e)

            def turn_prob(h):
                b = ps[:, 4, :].rearrange("p (k s) -> p k s", k=2)
                wait(PE, exped[h], pout.get(h - 1))
                for kt in range(2):
                    for th in range(2):
                        mm = PE.transpose(b[:, kt, th * P:(th + 1) * P], prob[:, h % 3, th, kt * P:(kt + 1) * P],
                                          ident[:])
                pturned[h] = pe.mark(mm)
                pout[h] = A(lambda: AC.activation(probT[:, h % 2, :], ps[:, 4, :], ACT.Copy), pturned[h])

            def mix(h):
                wait(PE, pout[h])
                if after is not None:
                    after.before_mix(h)
                for th in range(2):
                    for kt in range(2):
                        mm = PE.matmul(out_bank(h, th), probT[:, h % 2, kt * S + th * P:kt * S + (th + 1) * P],
                                       proj[:, kt, vcol(h):vcol(h) + dv], start=kt == 0, stop=kt == 1)
                mixed[h] = pe.mark(mm)
                if after is not None:
                    after(h, mixed[h])

            turn_qk(0)
            for i in range(n + 3):
                if i < n:
                    g = i // per_group + 1
                    if i % per_group == 0 and g * per_group < n:
                        turn_qk(g)
                    score(i)
                if i == 1 and begin is not None:
                    wait(PE, *begin())
                if fill is not None:
                    fill(i)
                if 2 <= i <= n + 1:
                    turn_prob(i - 2)
                if i >= 3:
                    mix(i - 3)
            return mixed[n - 1]

        def normalise(n, dv, col, done):
            a = V(lambda: DV.reciprocal(ri[:], rs[:]), done)
            for th in range(2):
                wait(DV, a)
                tk = V(lambda: DV.tensor_tensor(
                    proj[:, th, col:col + n * dv].rearrange("p (h d) -> p h d", h=n),
                    ps[:, 6 + th, 0:n * dv].rearrange("p (h d) -> p h d", h=n),
                    ri[:, :, th].unsqueeze(2).broadcast_to([P, n, dv]), ALU.mult))
            return tk

        def rotate(x1, x2, c, s, tmp1, tmp2, *toks):
            V(lambda: DV.tensor_tensor(tmp1, x1, s, ALU.mult), *toks)
            a = V(lambda: DV.tensor_tensor(tmp2, x2, s, ALU.mult), *toks)
            wait(DV, a)
            V(lambda: DV.tensor_tensor(x1, x1, c, ALU.mult))
            b = V(lambda: DV.tensor_tensor(x2, x2, c, ALU.mult))
            wait(DV, b)
            V(lambda: DV.tensor_tensor(x1, x1, tmp2, ALU.subtract))
            return V(lambda: DV.tensor_tensor(x2, x2, tmp1, ALU.add))

        def spread(ap, shape, axis=1):
            return ap.unsqueeze(axis).broadcast_to(shape)

        s_x.mark(SP.dma_start(x[:], t["x"][0].rearrange("(h p) c -> p h c", p=P)))
        x_in = s_x.now()
        s_vec.mark(AC.dma_start(vec[:, 0:D], t["ln_g"][0:1, :].broadcast_to([P, D])))
        s_vec.mark(AC.dma_start(vec[:, D:2 * D], t["ln_b"][0:1, :].broadcast_to([P, D])))
        for dst, src in ((ident[:], t["ident"]), (flip8[:], t["flip8"]), (gate[:, 0, 0:S], t["mask"]),
                         (rope[:], t["rope"].rearrange("(h p) c -> p h c", p=P))):
            s_par.mark(SP.dma_start(dst, src))
        V(lambda: DV.memset(half[:], -0.5))
        for th in range(2):
            norm_stats(th, x_in, dve.now())
        wait(DV, s_par.now())
        V(lambda: DV.tensor_copy(maskb[:], gate[:, 0, 0:S]))
        V(lambda: DV.tensor_copy(identb[:], ident[:]))
        wait(AC, dve.now())
        A(lambda: AC.activation(small[:, 60:61], half[:, 0:1], ACT.Exp))
        wait(PE, dve.now())
        pe.mark(PE.transpose(ps[:, 0, 0:P], ident[:], ident[:]))
        wait(PO, dve.now())
        G(lambda: PO.tensor_copy(small[:, 61:62], half[:, 0:1]))

        def ffn(w_in, w_out, L, first, second, out_banks_read, halves, early=False):
            wi = w_in[L].rearrange("(k p) n -> p k n", p=P)
            wo = w_out[L].rearrange("(k p) n -> p k n", p=P)

            def load_up(c):
                for k in (0, 4):
                    load_piece(wi[:, k:k + 4, bass.ds(c * FC, FC)], 4, 2 * FC,
                               wi[:, k:k + 4, bass.ds(c * FC + FF, FC)])

            def up(c, splits, ready=()):
                done = multiply(0, (4, 4), wide((0, 1), 2 * FC), 2 * FC, (xTh, xTl), ready=ready)
                catch_up(1)
                first(c, done[1])
                if splits > 1:
                    catch_up()

            def step(c, start, splits=3):
                free, stationary = out_banks_read(), dve.now()
                load_up(c)
                wait(PE, free)
                up(c, splits)
                load_piece(wo[:, bass.ds((c - 1) * 2, 2), :], 2, D)

                def down():
                    wait(PE, stationary)
                    return multiply(0, (2,), narrow, 512, (aTh, aTl), first=start, last=False, keep=splits < 2)

                if splits > 2 or not early:
                    down()
                    second(c, splits > 2, lambda: None)
                else:
                    second(c, False, down)

            load_up(0)
            up(0, 2, halves)
            second(0, False, lambda: None)
            step(1, True)
            with prog.loop("ffn%d" % len(prog.ffns), NSTEP - 3) as j:
                step(j + 2, False)
            prog.ffns.append(1)
            step(NSTEP - 1, False, 1)
            load_piece(wo[:, 2 * NSTEP - 2:2 * NSTEP, :], 2, D)
            wait(PE, dve.now())
            return multiply(0, (2,), narrow, 512, (aTh, aTl), first=False, keep=2)

        def narrow_gemm(w, groups, stat, ready=()):
            wv = w.rearrange("(k p) n -> p k n", p=P)
            kt = 0
            for i, sizes in enumerate(groups):
                kt1 = kt
                for kts in sizes:
                    load_piece(wv[:, kt1:kt1 + kts, :], kts, D)
                    kt1 += kts
                done = multiply(kt, sizes, narrow, 512, stat, i == 0, i == len(groups) - 1,
                                ready if i == 0 else ())
                kt = kt1
            return done

        down = ps[:, 4:8, :].rearrange("p (t n) w -> p t (n w)", t=2)
        EIGHT = ((2, 2), (1, 1), (1, 1))

        def halves(src, ready, scale=1.0, between=(None, None)):
            def first_half():
                r = ready[0]()
                between[0]()
                return turn_half(src, 0, (r,), scale)

            def second_half():
                between[1]()
                r = ready[1]()
                return turn_half(src, 1, (r,), scale)
            return [first_half, second_half]

        with prog.loop("layer1", DEPTH) as L:
            top = [c.now() for c in (pe, act, dve, pool)]
            for _ in range(RING):
                split_hi()
            w1 = t["w_in"][L].rearrange("(k p) n -> p k n", p=P)
            s_bg2.mark(SP.dma_start(vec[:, 2 * D:3 * D], t["b_gate"][bass.ds(L, 1), 2 * D:3 * D].broadcast_to([P, D])))

            stats = (dve.now(), pool.now(), s_vec.now())

            def apply_top(th):
                a.append(norm_apply(th, *stats))
                return a[th]
            a = []
            wait(PO, *top)
            settle(PO)
            for r in range(4):
                for kr in range(4):
                    src = t["rpb"][L, 0:8, 7 - r + kr, 0:64]
                    ap = bass.AP(src.tensor, src.offset, [[1, 64], [15 * 127, 8], [1, 64]])
                    s_lay.mark(PO.dma_start(rpb[64 * (r % 2):64 * (r % 2) + 64, :, r // 2, kr * 64:(kr + 1) * 64], ap))
            s_lay.mark(PO.dma_start(pcol[:, 0:6], t["pcol1"][L]))
            s_lay.mark(PO.dma_start(lamc[:], t["lamc"][bass.ds(L, 1), :].broadcast_to([P, 2])))
            s_lay.mark(PO.dma_start(gate[:, 0, 0:256], t["lam"][bass.ds(L, 1), :].broadcast_to([P, 256])))
            def load_gate_bias():
                wait(PO, a[1])
                settle(PO)
                s_bg.mark(PO.dma_start(vec[:, 0:2 * D], t["b_gate"][bass.ds(L, 1), 0:2 * D].broadcast_to([P, 2 * D])))
            for k in (0, 4):
                load_piece(w1[:, k:k + 4, PROJ + GATE0:PROJ + GATE0 + 512], 4, 512)
            done = multiply(0, (4, 4), wide((6, 7), 512), 512, (xTh, xTl),
                            ready=halves(x_cols, [lambda: apply_top(0), lambda: apply_top(1)], between=(split_lo, split_lo)))
            load_gate_bias()
            split_lo()
            behind[0] = 2
            catch_up(1)
            g = gate[:, :, GATE0:GATE0 + 512]
            a = V(lambda: DV.tensor_tensor(g, ps[:, 6:8, :], spread(vec[:, GATE0:GATE0 + 512], [P, 2, 512]), ALU.add),
                  done[1], s_bg2.now())
            A(lambda: AC.activation(g, g, ACT.Tanh, scale=0.5), a)
            catch_up()

            with prog.loop("w_in1", 2) as it:
                for j in range(3):
                    c0 = it * 1536 + j * 512
                    for k in (0, 4):
                        load_piece(w1[:, k:k + 4, bass.ds(c0, 512)], 4, 512)
                    chunk(512, proj[:, :, bass.ds(c0, 512)])
            wide_out = s_ev.now()

            def latent_chunk(j, keep=0, cols=(PIECE, PIECE)):
                c0 = MLA_COL + j * 224
                for k in (0, 4):
                    load_piece(w1[:, k:k + 4, c0:c0 + 224], 4, 224)
                chunk(224, proj[:, :, c0:c0 + 224], keep, cols)

            latent_chunk(0, cols=(4 * 224, 4 * 224))
            C = NA_W
            rows = proj[:, :, C:C + 1024].rearrange("p t (h d) -> p t h d", d=64)
            tq = [scratch[:, i * S:(i + 1) * S].rearrange(
                "p (t h d) -> p t h d", t=2, h=16) for i in range(2)]
            rotate(rows[:, :, :, 0:8], rows[:, :, :, 8:16],
                   spread(rope[:, :, 0:8], [P, 2, 16, 8], 2), spread(rope[:, :, 8:16], [P, 2, 16, 8], 2),
                   tq[0], tq[1], dve.now(), wide_out)
            latent_chunk(1, cols=(4 * 224, PIECE))

            lv = gate[:, 0, 0:256].rearrange("p (a b d) -> p a b d", a=2, b=2)
            a = V(lambda: DV.tensor_tensor(gate[:, 1, 0:128].rearrange("p (a d) -> p a d", a=2),
                                           lv[:, :, 0, :], lv[:, :, 1, :], ALU.mult), s_lay.now())
            a = V(lambda: DV.tensor_reduce(small[:, 4:6], gate[:, 1, 0:128].rearrange("p (a d) -> p a d", a=2),
                                           AX.X, ALU.add), a)
            lam_exp = A(lambda: AC.activation(small[:, 6:8], small[:, 4:6], ACT.Exp), a)
            latent_chunk(2, 1)
            a = V(lambda: DV.scalar_tensor_tensor(out=small[:, 8:9], in0=small[:, 6:7], scalar=-1.0,
                                                  in1=small[:, 7:8], op0=ALU.mult, op1=ALU.add), lam_exp)
            a = V(lambda: DV.tensor_tensor(small[:, 8:9], small[:, 8:9], lamc[:, 0:1], ALU.subtract), a)
            a = V(lambda: DV.tensor_tensor(pcol[:, 6:7], pcol[:, 5:6], lamc[:, 1:2], ALU.mult), a)
            lam_done = a

            def gate_pieces():
                for j in range(12):
                    bank, c0 = gate_bank[0], j * 256
                    if GATE0 <= c0 < GATE0 + 512:
                        continue
                    load_piece(w1[:, :, c0 + PROJ:c0 + PROJ + 256], 8, 256)
                    wait(PE, gate_free[bank])
                    multiply(0, (8,), half_bank(bank, 256), 256, (xTh, xTl), keep=gate_bank[1])
                    g = gate[:, :, c0:c0 + 256]
                    a = V(lambda: DV.tensor_tensor(g, ps[:, bank, :].rearrange("p (t n) -> p t n", t=2),
                                                   spread(vec[:, c0:c0 + 256], [P, 2, 256]), ALU.add),
                          s_mm.now(), s_bg.now(), lam_done)
                    A(lambda: AC.activation(g, g, ACT.Tanh, scale=0.5), a)
                    gate_free[bank] = gate_read[0] = a
                    yield

            gate_bank, gate_free, gate_read = [5, 0], {5: s_ev.now(), 2: None}, [None]
            gates = gate_pieces()

            def fill(*steps):
                def step(i):
                    if i in steps:
                        next(gates)
                    if i in (3, 5, 8):
                        split_one()
                return step

            def branch(i, src, ready, outs_free, gain=None, free=None, between=None):
                a = turn(src, 4, aTh, aTl, gain=gain, ready=(ready,), free=free, hold=False)
                if between:
                    between()
                start = (act.now(), dve.now())
                wait(PE, a, *outs_free)
                done = narrow_gemm(t["w_branch"][L, i], ((2, 2),), (aTh, aTl))

                gated = act.now()

                def merge(th):
                    g = gate[:, th, i * D:(i + 1) * D]
                    a = V(lambda: DV.scalar_tensor_tensor(out=g, in0=g, scalar=1.0, in1=down[:, th], op0=ALU.add,
                                                          op1=ALU.mult), done[th], gated, *added)
                    gate_free[5] = a
                    if i == 1:
                        wait(PO, a)
                        settle(PO)
                        added.append(pool.mark(PO.tensor_tensor(gate[:, th, 0:D], gate[:, th, 0:D], g, ALU.add)))
                    if i == 2:
                        a = V(lambda: DV.tensor_tensor(gate[:, th, 0:D], gate[:, th, 0:D], g, ALU.add), a)
                    return a
                return start, merge

            added = []

            def gate_in_2():
                gate_bank[0] = 2
                next(gates)
                gate_bank[0] = 5
                return gate_free[2]

            def begin_with(work):
                def begin():
                    a = [w() for w in work]
                    gate_bank[1] = RING - 1
                    a = [a[-1], gate_in_2(), gate_free[5]]
                    gate_bank[1] = 0
                    return a
                return begin

            def na_bias(h, th, bank):
                PE.matmul(bank, flip8[:], rpb[:, h, th, :], start=False, stop=False)
                return PE.matmul(bank, identb[:], maskb[:], start=False, stop=True)

            def rms_rows(y, sq, ss, width, *toks):
                a = V(lambda: DV.tensor_tensor(sq, y, y, ALU.mult), *toks)
                return V(lambda: DV.tensor_reduce(ss, sq, AX.X, ALU.add), a)

            def latent_norms():
                for col, wd, o, free in ((MLA_COL, MLA_Q, 24, D), (MLA_COL + MLA_Q, MLA_KV, 26, D + MLA_Q)):
                    y = proj[:, :, col:col + wd]
                    ss = small[:, o:o + 2]
                    for th in range(2):
                        a = A(lambda: AC.activation(gate[:, th, free:free + wd], y[:, th, :], ACT.Square,
                                                    accum_out=small[:, o + th:o + th + 1]), projected)
                    r = rsqrt(ss, ss, 1.0 / wd, RMS_EPS, a)
                    for th in range(2):
                        wait(DV, r)
                        a = V(lambda: DV.tensor_scalar(y[:, th, :], y[:, th, :], small[:, o + th:o + th + 1], None,
                                                       ALU.mult))
                return a

            projected = s_ev.now()
            wait(PE, s_lay.now())
            done = attention(8, True, lambda g: 128 * g, lambda g: 512 + 128 * g, 64,
                             lambda h: 1024 + 64 * h, 64, 0.125,
                             lambda h, th: ps[:, 6 + th, 64 * h:64 * h + 64], (projected, act.now()),
                             bias=na_bias, begin=begin_with([latent_norms]), fill=fill(5, 8))
            a = normalise(8, 64, 0, done)
            free = (act.now(), dve.now())
            start, merge = branch(0, lambda k, th: proj[:, th, k * P:(k + 1) * P], a, (a, gate_free[5]), free=free,
                                  between=gate_in_2)

            normed = {}

            class Diff:
                def before_mix(self, h):
                    wait(PE, normed.get(h // 2 - 2))

                def __call__(self, h, done):
                    if h % 2 == 0:
                        return
                    hd = h // 2
                    o = ps[:, 6 + hd % 2, :].rearrange("p (t j d) -> p t j d", t=2, j=2)
                    a = V(lambda: DV.reciprocal(ri[:, 0:2, :], rs[:, h - 1:h + 1, :]), done)
                    b = V(lambda: DV.tensor_scalar(ri[:, 2, :], ri[:, 1, :], small[:, 8:9], None, ALU.mult), a)
                    for th in range(2):
                        y = proj[:, th, C + hd * P:C + (hd + 1) * P]
                        c = V(lambda: DV.tensor_scalar(y, o[:, th, 0, :], ri[:, 0, th:th + 1], None, ALU.mult), b)
                    for th in range(2):
                        y = proj[:, th, C + hd * P:C + (hd + 1) * P]
                        normed[hd] = V(lambda: DV.scalar_tensor_tensor(
                            out=y, in0=o[:, th, 1, :], scalar=ri[:, 2, th:th + 1], in1=y, op0=ALU.mult,
                            op1=ALU.add), c)

            attention(8, True, lambda g: C + 128 * g, lambda g: C + 512 + 128 * g, 64,
                      lambda h: C + 1024 + 128 * (h // 2), 128, 0.125,
                      lambda h, th: ps[:, 6 + (h // 2) % 2, (th * 2 + h % 2) * P:(th * 2 + h % 2 + 1) * P],
                      start, after=Diff(), begin=begin_with([lambda: merge(0), lambda: merge(1)]), fill=fill(8))

            attn_end = (act.now(), dve.now())
            y = proj[:, :, C:C + 512].rearrange("p t (h d) -> p t h d", d=P)
            sq = scratch[:, 0:1024].rearrange("p (t h d) -> p t h d", t=2, h=4)
            ss = small[:, 16:24].rearrange("p (t h) -> p t h", t=2)
            a = rms_rows(y, sq, ss, P, pe.now(), dve.now())
            r = rsqrt(ss, ss, 1.0 / P, RMS_EPS, a)
            normed_df = V(lambda: DV.tensor_tensor(y, y, ss.unsqueeze(3).broadcast_to([P, 2, 4, P]), ALU.mult), r)

            turn(lambda k, th: proj[:, th, MLA_COL + k * P:MLA_COL + (k + 1) * P], 3, aTh, aTl,
                 gain=lambda k: pcol[:, k:k + 1], free=attn_end, hold=False)
            a = turn(lambda k, th: proj[:, th, MLA_COL + MLA_Q + k * P:MLA_COL + MLA_Q + (k + 1) * P], 2, aTh, aTl,
                     koff=3, bank0=2, gain=lambda k: pcol[:, 3 + k:4 + k], free=attn_end, hold=False)
            next(gates)
            wait(PE, a)
            wq = t["w_mla_qb"][L].rearrange("(k p) n -> p k n", p=P)
            for c0, wd, banks in ((0, 512, (0, 1)), (512, 256, (2, 3))):
                load_piece(wq[:, :, c0:c0 + wd], 3, wd)
                done = multiply(0, (3,), wide(banks, wd), wd, (aTh, aTl))
                A(lambda: AC.activation(proj[:, :, c0:c0 + wd], ps[:, banks[0]:banks[0] + 2, 0:wd], ACT.Copy),
                  done[1])
            q_out = act.now()
            load_piece(t["w_mla_kvb"][L].rearrange("(k p) n -> p k n", p=P), 2, D)
            wait(PE, *attn_end, gate_free[5])
            kv_done = multiply(0, (2,), narrow, 512, (aTh, aTl), toff=3)[1]
            kv = down.rearrange("p t (h e) -> p t h e", e=P)
            kf = proj[:, :, 768:1536].rearrange("p t (h e) -> p t h e", e=96)
            vf = proj[:, :, 1536:2048].rearrange("p t (h e) -> p t h e", e=64)
            for th in range(2):
                k_out = A(lambda: AC.activation(kf[:, th, :, 0:64], kv[:, th, :, 0:64], ACT.Copy), kv_done)

            v_done = [k_out]

            def latent_rest():
                for th in range(2):
                    v_out = V(lambda: DV.tensor_copy(vf[:, th], kv[:, th, :, 64:128]), kv_done, k_out, pe.now())
                v_done.append(v_out)
                gate_free[2] = q_out
                gate_in_2()
                tq = [scratch[:, i * S:(i + 1) * S].rearrange(
                    "p (t h d) -> p t h d", t=2, h=8) for i in range(2)]
                qf = proj[:, :, 0:768].rearrange("p t (h e) -> p t h e", e=96)
                cs, sn = rope[:, :, 16:32], rope[:, :, 32:48]
                rotate(qf[:, :, :, 64:80], qf[:, :, :, 80:96], spread(cs, [P, 2, 8, 16], 2),
                       spread(sn, [P, 2, 8, 16], 2), tq[0], tq[1], q_out)
                kr = proj[:, :, PROJ - MLA_R:PROJ]
                a = rotate(kr[:, :, 0:16], kr[:, :, 16:32], cs, sn, tq[0][:, :, 0, :], tq[1][:, :, 0, :],
                           dve.now())
                wait(DV, a)
                for th in range(2):
                    V(lambda: DV.tensor_copy(kf[:, th, :, 64:96], spread(kr[:, th, :], [P, 8, 32])))

            start, merge = branch(1, lambda k, th: proj[:, th, C + k * P:C + (k + 1) * P], normed_df, v_done,
                                  gain=lambda k: pcol[:, 6:7], free=(q_out,), between=latent_rest)
            done = attention(8, False, lambda h: 96 * h, lambda h: 768 + 96 * h, 96,
                             lambda h: 1536 + 64 * h, 64, 96 ** -0.5,
                             lambda h, th: ps[:, 6 + th, 64 * h:64 * h + 64], start,
                             begin=begin_with([lambda: merge(0), lambda: merge(1)]), fill=fill())
            a = normalise(8, 64, 0, done)
            _, merge = branch(2, lambda k, th: proj[:, th, k * P:(k + 1) * P], a, (a, gate_free[5]),
                              between=gate_in_2)
            assert next(gates, 0) == 0

            done = narrow_gemm(t["w_out"][L], EIGHT, (xTh, xTl),
                               ready=halves(lambda k, th: gate[:, th, k * P:(k + 1) * P],
                                            [lambda: merge(0), lambda: merge(1)], 0.5, (split_one, split_one)))

            def add_down(done, alpha, th):
                return V(lambda: DV.scalar_tensor_tensor(out=x[:, th], in0=x[:, th], scalar=alpha, in1=down[:, th],
                                                         op0=ALU.mult, op1=ALU.add), done, pe.now())

            wait(SP, *gate_read)
            s_vec.mark(SP.dma_start(vec[:, 0:D], t["ln1_g"][bass.ds(L, 1), :].broadcast_to([P, D])))
            s_vec.mark(SP.dma_start(vec[:, D:2 * D], t["ln1_b"][bass.ds(L, 1), :].broadcast_to([P, D])))
            stats1 = [norm_stats(th, add_down(done[th], ALPHA, th)) for th in range(2)]
            ln1_in, ln1_done = s_vec.now(), []

            def apply_ln1(th):
                ln1_done.append(norm_apply(th, stats1[th], ln1_in))
                return ln1_done[th]

            hid = gate[:, :, 0:FC]

            def first1(c, done):
                u = ps[:, 0:2, :]
                a = A(lambda: AC.activation(hid, u[:, :, 0:FC], ACT.Tanh, scale=0.5), done, pe.now())
                a = V(lambda: DV.scalar_tensor_tensor(out=hid, in0=hid, scalar=1.0, in1=u[:, :, 0:FC],
                                                      op0=ALU.add, op1=ALU.mult), a)
                V(lambda: DV.scalar_tensor_tensor(out=hid, in0=hid, scalar=0.5, in1=u[:, :, FC:2 * FC],
                                                  op0=ALU.mult, op1=ALU.mult), a)

            def second1(c, split, middle):
                b = ps[:, 2, :].rearrange("p (k s) -> p k s", k=2)
                wait(PE, dve.now())
                for k in range(2):
                    for th in range(2):
                        mm = PE.transpose(b[:, k, th * P:(th + 1) * P], gate[:, th, k * P:(k + 1) * P], ident[:])
                tt = pe.mark(mm)
                a = A(lambda: AC.activation(aTh[:, 0:2, :], b, ACT.Copy), tt)
                V(lambda: DV.tensor_tensor(aTl[:, 0:2, :], b, aTh[:, 0:2, :].bitcast(F32), ALU.subtract), a)
                if split:
                    catch_up()

            done = ffn(t["w_ffn_in"], t["w_ffn_out"], L, first1, second1, lambda: dve.now(back=1),
                       halves(x_cols, [lambda: apply_ln1(0), lambda: apply_ln1(1)], between=(split_one, split_one)))
            wait(SP, ln1_done[1])
            s_vec.mark(SP.dma_start(vec[:, 0:D], t["ln_g"][bass.ds(L + 1, 1), :].broadcast_to([P, D])))
            s_vec.mark(SP.dma_start(vec[:, D:2 * D], t["ln_b"][bass.ds(L + 1, 1), :].broadcast_to([P, D])))
            for th in range(2):
                norm_stats(th, add_down(done[th], ALPHA, th))
        assert n_mm.static() % RING == 0 and n_split.static() == n_mm.static() == n_dma.static()

        ln2 = (dve.now(), pool.now(), s_vec.now())
        for th in range(2):
            norm_apply(th, *ln2)

        scr = gate
        flat = rpb[:].rearrange("p a b c -> p (a b c)")
        cw = flat[:, 0:NSTEP * 16].rearrange("p (c f k) -> p c f k", c=NSTEP, f=4)
        sgw = flat[:, D:2 * D].rearrange("p (h q) -> p h q", h=8)
        brow = flat[:, 2 * D:3 * D + 640]

        def load_parameters(l):
            for dst, src in ((pcol[:, 0:16], t["pcol2"][l]), (sgw, t["sgw"][l]),
                             (brow, t["brow2"][bass.ds(l, 1), :].broadcast_to([P, D + 640]))):
                s_par.mark(SP.dma_start(dst, src))

        load_parameters(0)
        with prog.loop("layer2", DEPTH) as L:
            top = [c.now() for c in (pe, act, dve, pool)]
            x_done = (dve.now(back=1), dve.now())
            for _ in range(RING):
                split_hi()

            def halves2(src, ready, between):
                return halves(src, [lambda r=r: r for r in ready], between=(lambda: None, between))

            def rms_scale(y, dst, width, o, *toks):
                for th in range(2):
                    a = A(lambda: AC.activation(scr[:, th, 2 * D:2 * D + width], y[:, th, :], ACT.Square,
                                                accum_out=small[:, o + th:o + th + 1]), *toks)
                r = rsqrt(small[:, o:o + 2], small[:, o:o + 2], 1.0 / width, RMS_EPS, a)
                wait(DV, r)
                for th in range(2):
                    a = V(lambda: DV.tensor_scalar(dst[:, th, :], y[:, th, :], small[:, o + th:o + th + 1], None,
                                                   ALU.mult))
                return a

            w2 = t["w_in_2"][L].rearrange("(k p) n -> p k n", p=P)
            def rms_x(gain, o, *toks, mid=lambda: None):
                r = []
                for th in range(2):
                    a = A(lambda: AC.activation(scr[:, th, 2 * D:3 * D], x[:, th, :], ACT.Square,
                                                accum_out=small[:, o + th:o + th + 1]), toks[th])
                    r.append(rsqrt(small[:, o + th:o + th + 1], small[:, o + th:o + th + 1], 1.0 / D, RMS_EPS, a))
                mid()
                return [V(lambda: DV.scalar_tensor_tensor(out=scr[:, th, 0:D], in0=x[:, th, :],
                                                          scalar=small[:, o + th:o + th + 1],
                                                          in1=gain, op0=ALU.mult, op1=ALU.mult),
                          r[th], s_par.now()) for th in range(2)]

            def scr_cols(k, th):
                return scr[:, th, k * P:(k + 1) * P]

            before = (pe.now(), act.now())
            wait(AC, *before)
            a = rms_x(brow[:, 0:D], 0, x_done[0], x_done[1], mid=split_lo)
            wait(DV, s_par.now())
            wait(AC, s_par.now())

            def project(c0, wd, banks, func=ACT.Copy, between=lambda: None, ready=()):
                for k in (0, 4):
                    load_piece(w2[:, k:k + 4, c0:c0 + wd], 4, wd)
                done = multiply(0, (4, 4), wide(banks, wd), wd, (xTh, xTl), ready=ready)
                if ready:
                    split_lo()
                    behind[0] = 2
                catch_up(1)
                between()
                A(lambda: AC.activation(proj[:, :, c0:c0 + wd], ps[:, banks[0]:banks[0] + 2, 0:wd], func), done[1])
                catch_up()
                between()

            project(0, 512, (4, 5), ready=halves2(scr_cols, a, split_lo))
            project(512, 256, (6, 7))

            y = proj[:, :, 0:640]
            yh = y.rearrange("p t (h d) -> p t h d", d=64)
            sq = scr[:, :, 0:640].rearrange("p t (h d) -> p t h d", d=64)
            ssq = small[:, 32:52].rearrange("p (t h) -> p t h", t=2)

            def norm_qk():
                a = V(lambda: DV.tensor_tensor(sq, yh, yh, ALU.mult), qkv_out, xt_done)
                a = V(lambda: DV.tensor_reduce(ssq, sq, AX.X, ALU.add), a)
                a = G(lambda: PO.tensor_scalar(ssq, ssq, 1.0 / 64, RMS_EPS, ALU.mult, ALU.add), a)
                for th in range(2):
                    wait(PO, a)
                    settle(PO)
                    r = G(lambda: PO.tensor_tensor(ssq[:, th, :], ssq[:, th, :], half[:, 0:10], ALU.pow))
                yield
                wait(DV, r)
                for th in range(2):
                    a = V(lambda: DV.tensor_tensor(yh[:, th], yh[:, th],
                                                   ssq[:, th, :].unsqueeze(2).broadcast_to([P, 10, 64]), ALU.mult))
                wait(DV, a)
                for th in range(2):
                    a = V(lambda: DV.tensor_tensor(yh[:, th, 0:8], yh[:, th, 0:8], spread(brow[:, D:D + 64], [P, 8, 64]),
                                                   ALU.mult))
                    a = V(lambda: DV.tensor_tensor(yh[:, th, 8:10], yh[:, th, 8:10],
                                                   spread(brow[:, D + 64:D + 128], [P, 2, 64]), ALU.mult))
                yield
                for th in range(2):
                    r4 = y[:, th, :].rearrange("p (h a z d) -> p h a z d", a=2, z=2, d=16)
                    c4 = rope[:, th, 48:80].rearrange("p (a d) -> p a d", a=2)
                    s4 = rope[:, th, 80:112].rearrange("p (a d) -> p a d", a=2)
                    tq = [scr[:, th, i * 320:(i + 1) * 320].rearrange("p (h a d) -> p h a d", h=10, a=2)
                          for i in (0, 1)]
                    rotate(r4[:, :, :, 0, :], r4[:, :, :, 1, :], spread(c4, [P, 10, 2, 16]),
                           spread(s4, [P, 10, 2, 16]), tq[0], tq[1], a)
                    yield

            qkv_out, xt_done = act.now(), pe.now()
            norm = norm_qk()
            next(norm)
            project(768, 512, (0, 1), ACT.Gelu_apprx_tanh, lambda: next(norm))
            project(1280, 512, (2, 3), ACT.Gelu_apprx_tanh, lambda: next(norm, None))
            uv_out = act.now()

            u, v = proj[:, :, 768:1280], proj[:, :, 1280:1792]
            vh = v.rearrange("p t (h d) -> p t h d", d=64)
            sv = scr[:, :, 1280:1792].rearrange("p t (h d) -> p t h d", d=64)
            ssv = small[:, 0:16].rearrange("p (t h) -> p t h", t=2)

            def gating():
                a = V(lambda: DV.tensor_tensor(sv, vh, vh, ALU.mult), uv_out, pool.now())
                a = V(lambda: DV.tensor_reduce(ssv, sv, AX.X, ALU.add), a)
                r = rsqrt(ssv, ssv, 1.0 / 64, RMS_EPS, a)
                yield
                yield
                for th in range(2):
                    a = V(lambda: DV.tensor_tensor(vh[:, th], vh[:, th],
                                                   ssv[:, th, :].unsqueeze(2).broadcast_to([P, 8, 64]), ALU.mult), r)
                vn = V(lambda: DV.tensor_tensor(v, v, spread(brow[:, D + 128:D + 640], [P, 2, 512]), ALU.mult), a)
                a = None
                for g in range(2):
                    wait(PE, vn, a)
                    for h in range(4 * g, 4 * g + 4):
                        mm = PE.matmul(ps[:, 5, (h % 4) * P:(h % 4 + 1) * P].rearrange("p (t d) -> p t d", t=2),
                                       sgw[:, h, :], vh[:, :, h, :], start=True, stop=True)
                    tt = pe.mark(mm)
                    yield
                    mixed = ps[:, 5, :].rearrange("p (h t d) -> p t h d", h=4, t=2)
                    for th in range(2):
                        a = V(lambda: DV.tensor_tensor(
                            vh[:, th, 4 * g:4 * g + 4], mixed[:, th],
                            pcol[:, 8 + 4 * g:12 + 4 * g].unsqueeze(2).broadcast_to([P, 4, 64]), ALU.add), tt)
                a = V(lambda: DV.tensor_tensor(v, v, u, ALU.mult), a)
                yield
                rms_scale(v, scr[:, :, 512:1024], 512, 26, a, act.now())
                yield

            gate_steps = gating()
            done = attention(8, False, lambda h: 64 * h, lambda h: 512 + 64 * (h // 4), 64,
                             lambda h: 640 + 64 * (h // 4), 64, 0.125,
                             lambda h, th: ps[:, 6 + th, 64 * h:64 * h + 64], (act.now(), dve.now()),
                             fill=lambda i: next(gate_steps, None) if i else None)
            sg_done = dve.now()
            assert next(gate_steps, 0) == 0
            a = normalise(8, 64, 0, done)
            free = (act.now(), a)
            a = rms_scale(proj[:, :, 0:512], scr[:, :, 0:512], 512, 24, a, act.now())
            turn(lambda k, th: scr[:, th, (4 + k) * P:(5 + k) * P], 4, xTh, xTl, koff=4, bank0=2,
                 gain=lambda k: pcol[:, 4 + k:5 + k], ready=(sg_done,), free=free, hold=False)
            turn(lambda k, th: scr[:, th, k * P:(k + 1) * P], 4, xTh, xTl,
                 gain=lambda k: pcol[:, k:k + 1], ready=(a,), free=free)
            wait(SP, *top)
            settle(SP)
            s_par.mark(SP.dma_start(vec[:, 0:D], t["ffn_norm_g_2"][bass.ds(L, 1), :].broadcast_to([P, D])))
            s_par.mark(SP.dma_start(cw, t["conv"][L]))
            done = narrow_gemm(t["w_o_2"][L], ((2, 2), (2, 2)), (xTh, xTl))
            a = [V(lambda: DV.tensor_tensor(x[:, th], x[:, th], down[:, th], ALU.add), done[th]) for th in range(2)]
            a = rms_x(vec[:, 0:D], 28, *a)
            attention_done = a[1]

            up4 = scr[:, 0, 0:1024].rearrange("p (t n) -> p t n", t=2)
            conv = scr[:, 0, 1024:2048].rearrange("p (f s) -> p f s", f=4)
            act2 = scr[:, 0, 2048:2560].rearrange("p (f s) -> p f s", f=2)

            def first2(c, done):
                A(lambda: AC.activation(up4, ps[:, 0:2, :], ACT.Copy), done, pe.now())

            def second2(c, split, middle):
                turned = ps[:, 2:4, :].rearrange("p b (f s) -> p (b f) s", f=2)
                wait(PE, act.now(), dve.now())
                for f in range(4):
                    for th in range(2):
                        mm = PE.transpose(turned[:, f, th * P:(th + 1) * P], up4[:, th, f * P:(f + 1) * P], ident[:])
                tt = pe.mark(mm)
                middle()
                if split:
                    catch_up()
                product = s_mm.now()
                wait(AC, tt, dve.now())
                for f in range(4):
                    w = cw[:, c, f, :] if isinstance(c, int) else cw[:, bass.ds(c, 1), f, :].rearrange("p c k -> p (c k)")
                    a = A(lambda: AC.activation(conv[:, f, :], turned[:, f, :], ACT.Identity, bias=w[:, 3:4],
                                                scale=w[:, 1:2]))
                wait(DV, a)
                for k, dst, src in ((0, slice(1, S), slice(0, S - 1)), (2, slice(0, S - 1), slice(1, S))):
                    for f in range(4):
                        w = cw[:, c, f, :] if isinstance(c, int) else cw[:, bass.ds(c, 1), f, :].rearrange("p c k -> p (c k)")
                        a = V(lambda: DV.scalar_tensor_tensor(out=conv[:, f, dst], in0=turned[:, f, src],
                                                              scalar=w[:, k:k + 1], in1=conv[:, f, dst],
                                                              op0=ALU.mult, op1=ALU.add))
                    wait(DV, a)
                a = A(lambda: AC.activation(act2, conv[:, 0:2, :], ACT.Tanh, scale=0.5), a)
                a = V(lambda: DV.scalar_tensor_tensor(out=act2, in0=act2, scalar=1.0, in1=conv[:, 0:2, :],
                                                      op0=ALU.add, op1=ALU.mult), a)
                a = V(lambda: DV.scalar_tensor_tensor(out=act2, in0=act2, scalar=0.5, in1=conv[:, 2:4, :],
                                                      op0=ALU.mult, op1=ALU.mult), a)
                a = A(lambda: AC.activation(aTh[:, 0:2, :], act2, ACT.Copy), a, product)
                V(lambda: DV.tensor_tensor(aTl[:, 0:2, :], act2, aTh[:, 0:2, :].bitcast(F32), ALU.subtract), a)

            done = ffn(t["w_up_2"], t["w_down_2"], L, first2, second2, lambda: act.now(back=6),
                       halves2(scr_cols, a, catch_up), early=True)
            wait(SP, attention_done)
            load_parameters(L + 1)
            for th in range(2):
                V(lambda: DV.tensor_tensor(x[:, th], x[:, th], down[:, th], ALU.add), done[th], dve.now(back=th))

        wait(SP, dve.now())
        s_out.mark(SP.dma_start(out[0].rearrange("(h p) c -> p h c", p=P), x[:]))
        wait(SP, s_out.now(), s_par.now())
    return prog.wrong


def constants():
    import numpy as np
    ident = np.eye(P, dtype=np.float32)
    q = np.arange(64)
    flip = np.zeros((P, P), np.float32)
    for b in range(2):
        flip[64 * b + 63 - q, 64 * b + q] = 8.0
    start = np.clip(q - 8, 0, 48)[:, None]
    ok = (q[None, :] >= start) & (q[None, :] < start + 16)
    mask = np.where(np.tile(ok, (2, 4)), 0.0, -1e30).astype(np.float32)
    s = np.arange(S, dtype=np.float32)[:, None]

    def cs(half, theta):
        f = np.exp(-math.log(theta) * np.arange(half, dtype=np.float32) / half).astype(np.float32)
        a = (s * f[None, :]).astype(np.float32)
        return [np.cos(a), np.sin(a)]
    f = (1.0 / (10000.0 ** (np.arange(0, 32, 2, dtype=np.float32) / 32))).astype(np.float32)
    ar, ac = (s // 64) * f, (s % 64) * f
    rope = np.concatenate(cs(8, 500000.0) + cs(16, 500000.0)
                          + [np.cos(ar), np.cos(ac), np.sin(ar), np.sin(ac)], 1).astype(np.float32)
    init = [0.8 - 0.6 * math.exp(-0.3 * l) for l in range(DEPTH)]
    lamc = np.array([[i, 1.0 - i] for i in init], np.float32)
    return {"ident": ident, "flip8": flip, "mask": mask, "rope": rope, "lamc": lamc}


def lay_out(i):
    import numpy as np

    def cols(a):
        return a.reshape(DEPTH, -1, P).transpose(0, 2, 1)
    t = {k: i[k] for k in ("x", "w_in", "b_gate", "w_mla_qb", "w_mla_kvb", "w_branch", "w_out", "ln1_g", "ln1_b",
                           "w_ffn_in", "w_ffn_out", "w_in_2", "w_o_2", "w_up_2", "w_down_2")}
    t["ln_g"] = np.concatenate([i["ln_in_g"][None], i["ln2_g"]], 0)
    t["ln_b"] = np.concatenate([i["ln_in_b"][None], i["ln2_b"]], 0)
    rpb = np.zeros((DEPTH, 8, 15, 127), np.float32)
    rpb[..., 48:79] = i["na_rpb"]
    t["rpb"] = rpb
    t["lam"] = i["diff_lambda"].reshape(DEPTH, 256)
    t["pcol1"] = np.concatenate([cols(i["mla_q_norm_g"]), cols(i["mla_kv_norm_g"]), cols(i["diff_subln_g"])], 2)
    def one_more(a):
        return np.concatenate([a, np.zeros_like(a[:1])], 0)
    t["ffn_norm_g_2"] = i["ffn_norm_g_2"]
    t["pcol2"] = one_more(np.concatenate([cols(i["attn_out_g_2"]), cols(i["sg_out_g_2"]),
                                          i["sg_b_2"].transpose(0, 2, 1)], 2))
    t["brow2"] = one_more(np.concatenate([i["attn_norm_g_2"], i["q_norm_g_2"], i["k_norm_g_2"],
                                          i["sg_norm_g_2"].reshape(DEPTH, 512)], 1))
    t["sgw"] = one_more(i["sg_w_2"].transpose(0, 3, 1, 2))
    cw = np.concatenate([i["conv_w_2"], i["conv_b_2"][:, None]], 1)
    cw = cw.reshape(DEPTH, 4, 2, NSTEP, 2, P)
    t["conv"] = cw.transpose(0, 5, 3, 2, 4, 1).reshape(DEPTH, P, NSTEP, 4, 4)
    t.update(constants())
    return {k: np.ascontiguousarray(v) for k, v in t.items()}


def kernel(**inputs):
    import numpy as np
    import concourse.bacc as bacc
    from concourse.bass_utils import run_bass_kernel_spmd

    arrays = {"in_" + k: v for k, v in lay_out({k: np.asarray(v) for k, v in inputs.items()}).items()}
    nc = bacc.Bacc("TRN2", target_bir_lowering=False, num_devices=1)
    t = {k[3:]: nc.dram_tensor(k, v.shape, F32, kind="ExternalInput").ap() for k, v in arrays.items()}
    out = nc.dram_tensor("out_0", (1, S, D), F32, kind="ExternalOutput").ap()
    wrong = build(nc, t, out, PER)
    assert not wrong, wrong
    r = run_bass_kernel_spmd(nc, [arrays], core_ids=[0])
    return r.results[0]["out_0"]
```
